# Optimizing a Trainium2 kernel written in Bass

```python
import math
import jax
import jax.numpy as jnp
from jax import lax
import numpy as np

D_MODEL = 1024
BATCH = 1
SEQ = 256
DEPTH = 1

EPS = 1e-6
CONV_K = 4

SSD_D_INNER = 2 * D_MODEL
SSD_HEAD_DIM = 64
SSD_HEADS = SSD_D_INNER // SSD_HEAD_DIM
SSD_GROUPS = 4
SSD_STATE = 128
SSD_CHUNK = 128
SSD_XBC = SSD_D_INNER + 2 * SSD_GROUPS * SSD_STATE

GDN_HEADS = 8
GDN_HEAD_DIM = 128
GDN_DIM = GDN_HEADS * GDN_HEAD_DIM
GDN_CHUNK = 64

MOE_GROUPS = 4
MOE_EXPERTS_PER_GROUP = 4
MOE_EXPERTS = MOE_GROUPS * MOE_EXPERTS_PER_GROUP
MOE_TOP_K = 2
MOE_D_FF = 512

SPLIT_SIZES = (SSD_D_INNER, SSD_XBC, SSD_HEADS, 3 * GDN_DIM, GDN_HEADS, GDN_HEADS, GDN_DIM, 2 * D_MODEL)
IN_PROJ_DIM = SSD_D_INNER + SSD_XBC + SSD_HEADS + 3 * GDN_DIM + 2 * GDN_HEADS + GDN_DIM + 2 * D_MODEL

kernel_name = 'hybrid_ssd_gdn_hier_moe'

def split_points(sizes):
    return [int(v) for v in np.cumsum(sizes)[:-1]]

def rms_norm(x, w):
    xf = x.astype(jnp.float32)
    y = xf * lax.rsqrt(jnp.mean(xf * xf, axis=-1, keepdims=True) + EPS)
    return (y * w.astype(jnp.float32)).astype(x.dtype)

def l2_normalize(x):
    return x * lax.rsqrt(jnp.sum(x * x, axis=-1, keepdims=True) + EPS)

def causal_depthwise_conv(u, w):
    return lax.conv_general_dilated(
        u, w[:, None, :].astype(u.dtype), window_strides=(1,), padding=[(CONV_K - 1, 0)],
        dimension_numbers=('NWC', 'WIO', 'NWC'), feature_group_count=u.shape[-1])

def ssd_chunked(xh, dt, a, bm, cm):
    bsz, seqlen, nh, hp = xh.shape
    ng, ns = bm.shape[2], bm.shape[3]
    r = nh // ng
    nc = seqlen // SSD_CHUNK
    q = SSD_CHUNK
    x = (xh * dt[..., None]).reshape(bsz, nc, q, ng, r, hp)
    a_cs = jnp.cumsum((dt * a).reshape(bsz, nc, q, ng, r), axis=2)
    bc = bm.reshape(bsz, nc, q, ng, ns)
    cc = cm.reshape(bsz, nc, q, ng, ns)
    at = jnp.moveaxis(a_cs, 2, -1)
    causal = jnp.tril(jnp.ones((q, q), dtype=bool))
    seg = at[..., :, None] - at[..., None, :]
    lmat = jnp.exp(jnp.where(causal, seg, -jnp.inf))
    scores = jnp.einsum('bclgn,bcsgn->bcgls', cc, bc)
    y_diag = jnp.einsum('bcgrls,bcsgrp->bclgrp', scores[:, :, :, None] * lmat, x)
    decay_to_end = jnp.moveaxis(jnp.exp(at[..., -1:] - at), -1, 2)
    states = jnp.einsum('bcsgn,bcsgrp->bcgrpn', bc, x * decay_to_end[..., None])
    chunk_decay = jnp.exp(at[..., -1])

    def step(hstate, inp):
        st, dec = inp
        return hstate * dec[..., None, None] + st, hstate

    h0 = jnp.zeros((bsz, ng, r, hp, ns), xh.dtype)
    _, prev = lax.scan(step, h0, (jnp.swapaxes(states, 0, 1), jnp.swapaxes(chunk_decay, 0, 1)))
    prev = jnp.swapaxes(prev, 0, 1)
    y_off = jnp.einsum('bclgn,bcgrpn->bclgrp', cc, prev) * jnp.exp(a_cs)[..., None]
    return (y_diag + y_off).reshape(bsz, seqlen, nh, hp)

def gated_delta_chunked(q, k, v, log_decay, beta):
    bsz, seqlen, nh, hd = q.shape
    nc = seqlen // GDN_CHUNK
    c = GDN_CHUNK

    def to_chunks(t):
        return t.reshape(bsz, nc, c, nh, -1).transpose(0, 1, 3, 2, 4)

    qc, kc, vc = to_chunks(q), to_chunks(k), to_chunks(v)
    gc = jnp.cumsum(log_decay.reshape(bsz, nc, c, nh).transpose(0, 1, 3, 2), axis=-1)
    bc = beta.reshape(bsz, nc, c, nh).transpose(0, 1, 3, 2)[..., None]
    incl = jnp.tril(jnp.ones((c, c), dtype=bool))
    strict = jnp.tril(jnp.ones((c, c), dtype=bool), -1)
    decay = jnp.exp(jnp.where(incl, gc[..., :, None] - gc[..., None, :], -jnp.inf))
    kb = kc * bc
    m = jnp.where(strict, jnp.einsum('bchid,bchjd->bchij', kb, kc) * decay, 0.0)
    eye = jnp.eye(c, dtype=q.dtype)
    t_inv = lax.linalg.triangular_solve(eye + m, jnp.broadcast_to(eye, m.shape),
                                        left_side=True, lower=True, unit_diagonal=True)
    u = t_inv @ (vc * bc)
    w = t_inv @ (kb * jnp.exp(gc)[..., None])
    a_qk = jnp.einsum('bchid,bchjd->bchij', qc, kc) * decay
    g_last = gc[..., -1]
    k_dec = kc * jnp.exp(g_last[..., None] - gc)[..., None]
    q_dec = qc * jnp.exp(gc)[..., None]

    def step(s, inp):
        qd, kd, uu, ww, aqk, gl = inp
        v_new = uu - ww @ s
        o = qd @ s + aqk @ v_new
        s = s * jnp.exp(gl)[..., None, None] + jnp.swapaxes(kd, -1, -2) @ v_new
        return s, o

    s0 = jnp.zeros((bsz, nh, hd, vc.shape[-1]), q.dtype)
    xs = (jnp.swapaxes(q_dec, 0, 1), jnp.swapaxes(k_dec, 0, 1), jnp.swapaxes(u, 0, 1),
          jnp.swapaxes(w, 0, 1), jnp.swapaxes(a_qk, 0, 1), jnp.swapaxes(g_last, 0, 1))
    _, o = lax.scan(step, s0, xs)
    return o.transpose(1, 0, 3, 2, 4).reshape(bsz, seqlen, nh, -1)

def mixer_block(u, w_in, ssd_conv_w, ssd_conv_b, ssd_dt_bias, ssd_a_log, ssd_d, ssd_norm_w, w_ssd_proj,
                gdn_conv_w, gdn_dt_bias, gdn_a_log, gdn_norm_w, w_gdn_proj, b_merge, w_out):
    bsz, seqlen, _ = u.shape
    f32 = jnp.float32
    proj = u @ w_in
    z_s, xbc_s, dt_s, qkv_g, a_g, beta_g, z_g, gate_pre = jnp.split(proj, split_points(SPLIT_SIZES), axis=-1)

    xbc = jax.nn.silu(causal_depthwise_conv(xbc_s, ssd_conv_w) + ssd_conv_b.astype(u.dtype)).astype(f32)
    xs, bs, cs = jnp.split(xbc, [SSD_D_INNER, SSD_D_INNER + SSD_GROUPS * SSD_STATE], axis=-1)
    xh = xs.reshape(bsz, seqlen, SSD_HEADS, SSD_HEAD_DIM)
    dt = jax.nn.softplus(dt_s.astype(f32) + ssd_dt_bias.astype(f32))
    a = -jnp.exp(ssd_a_log.astype(f32))
    y = ssd_chunked(xh, dt, a, bs.reshape(bsz, seqlen, SSD_GROUPS, SSD_STATE),
                    cs.reshape(bsz, seqlen, SSD_GROUPS, SSD_STATE))
    y = y + ssd_d.astype(f32)[:, None] * xh
    y = rms_norm(y.reshape(bsz, seqlen, SSD_D_INNER) * jax.nn.silu(z_s.astype(f32)), ssd_norm_w)
    y_ssd = y.astype(u.dtype) @ w_ssd_proj

    qkv = jax.nn.silu(causal_depthwise_conv(qkv_g, gdn_conv_w)).astype(f32)
    q, k, v = [t.reshape(bsz, seqlen, GDN_HEADS, GDN_HEAD_DIM) for t in jnp.split(qkv, 3, axis=-1)]
    q = l2_normalize(q) * GDN_HEAD_DIM ** -0.5
    k = l2_normalize(k)
    log_decay = -jnp.exp(gdn_a_log.astype(f32)) * jax.nn.softplus(a_g.astype(f32) + gdn_dt_bias.astype(f32))
    beta = jax.nn.sigmoid(beta_g.astype(f32))
    o = gated_delta_chunked(q, k, v, log_decay, beta)
    o = rms_norm(o, gdn_norm_w) * jax.nn.silu(z_g.astype(f32).reshape(bsz, seqlen, GDN_HEADS, GDN_HEAD_DIM))
    y_gdn = o.reshape(bsz, seqlen, GDN_DIM).astype(u.dtype) @ w_gdn_proj

    gates = jax.nn.sigmoid(gate_pre.astype(f32) + b_merge.astype(f32))
    g_ssd, g_gdn = jnp.split(gates, 2, axis=-1)
    merged = (g_ssd * y_ssd.astype(f32) + g_gdn * y_gdn.astype(f32)).astype(u.dtype)
    return merged @ w_out

def hierarchical_moe(u, w_group, b_group, w_expert, b_expert, w_gate, w_up, w_down):
    bsz, seqlen, d = u.shape
    f32 = jnp.float32
    t = u.reshape(-1, d)
    n = t.shape[0]
    group_logits = (t @ w_group).astype(f32) + b_group.astype(f32)
    group_prob = jax.nn.softmax(group_logits, axis=-1)
    _, gsel = lax.top_k(group_logits, 1)
    group_w = jnp.take_along_axis(group_prob, gsel, axis=-1)
    exp_logits = ((t @ w_expert).astype(f32) + b_expert.astype(f32)).reshape(n, MOE_GROUPS, MOE_EXPERTS_PER_GROUP)
    sel_logits = jnp.take_along_axis(exp_logits, gsel[:, :, None], axis=1)[:, 0]
    exp_prob = jax.nn.softmax(sel_logits, axis=-1)
    top_p, top_i = lax.top_k(exp_prob, MOE_TOP_K)
    top_p = top_p / jnp.sum(top_p, axis=-1, keepdims=True)
    expert_idx = gsel * MOE_EXPERTS_PER_GROUP + top_i
    combine = jnp.sum(jax.nn.one_hot(expert_idx, MOE_EXPERTS, dtype=f32) * (group_w * top_p)[..., None], axis=1)
    h_gate = jnp.einsum('td,edf->tef', t, w_gate)
    h_up = jnp.einsum('td,edf->tef', t, w_up)
    h = jax.nn.silu(h_gate) * h_up * combine.astype(t.dtype)[..., None]
    y = jnp.einsum('tef,efd->td', h, w_down)
    return y.reshape(bsz, seqlen, d)

def setup_inputs(seed: int = 0) -> dict:
    key = jax.random.key(seed)
    ks = jax.random.split(key, 32)
    f32 = jnp.float32

    def dense(k, shape, fan_in):
        return jax.random.normal(k, shape, f32) * fan_in ** -0.5

    def gain(k, shape):
        return 1.0 + 0.02 * jax.random.normal(k, shape, f32)

    def small(k, shape, scale=0.02):
        return scale * jax.random.normal(k, shape, f32)

    def dt_bias(k, shape):
        dt = jnp.exp(jax.random.uniform(k, shape, f32, math.log(1e-3), math.log(1e-1)))
        return dt + jnp.log(-jnp.expm1(-dt))

    def a_log(k, shape):
        return jnp.log(jax.random.uniform(k, shape, f32, 1.0, 16.0))

    return {
        'x': jax.random.normal(ks[0], (BATCH, SEQ, D_MODEL), f32),
        'ln1_w': gain(ks[1], (DEPTH, D_MODEL)),
        'w_in': dense(ks[2], (DEPTH, D_MODEL, IN_PROJ_DIM), D_MODEL),
        'ssd_conv_w': dense(ks[3], (DEPTH, CONV_K, SSD_XBC), CONV_K),
        'ssd_conv_b': small(ks[4], (DEPTH, SSD_XBC)),
        'ssd_dt_bias': dt_bias(ks[5], (DEPTH, SSD_HEADS)),
        'ssd_a_log': a_log(ks[6], (DEPTH, SSD_HEADS)),
        'ssd_d': gain(ks[7], (DEPTH, SSD_HEADS)),
        'ssd_norm_w': gain(ks[8], (DEPTH, SSD_D_INNER)),
        'w_ssd_proj': dense(ks[9], (DEPTH, SSD_D_INNER, D_MODEL), SSD_D_INNER),
        'gdn_conv_w': dense(ks[10], (DEPTH, CONV_K, 3 * GDN_DIM), CONV_K),
        'gdn_dt_bias': dt_bias(ks[11], (DEPTH, GDN_HEADS)),
        'gdn_a_log': a_log(ks[12], (DEPTH, GDN_HEADS)),
        'gdn_norm_w': gain(ks[13], (DEPTH, GDN_HEAD_DIM)),
        'w_gdn_proj': dense(ks[14], (DEPTH, GDN_DIM, D_MODEL), GDN_DIM),
        'b_merge': small(ks[15], (DEPTH, 2 * D_MODEL)),
        'w_out': dense(ks[16], (DEPTH, D_MODEL, D_MODEL), D_MODEL),
        'ln2_w': gain(ks[17], (DEPTH, D_MODEL)),
        'moe_w_group': dense(ks[18], (DEPTH, D_MODEL, MOE_GROUPS), D_MODEL),
        'moe_b_group': small(ks[19], (DEPTH, MOE_GROUPS), 0.01),
        'moe_w_expert': dense(ks[20], (DEPTH, D_MODEL, MOE_EXPERTS), D_MODEL),
        'moe_b_expert': small(ks[21], (DEPTH, MOE_EXPERTS), 0.01),
        'moe_w_gate': dense(ks[22], (DEPTH, MOE_EXPERTS, D_MODEL, MOE_D_FF), D_MODEL),
        'moe_w_up': dense(ks[23], (DEPTH, MOE_EXPERTS, D_MODEL, MOE_D_FF), D_MODEL),
        'moe_w_down': dense(ks[24], (DEPTH, MOE_EXPERTS, MOE_D_FF, D_MODEL), MOE_D_FF),
        'final_norm_w': gain(ks[25], (D_MODEL,)),
    }

def reference(x, ln1_w, w_in, ssd_conv_w, ssd_conv_b, ssd_dt_bias, ssd_a_log, ssd_d, ssd_norm_w, w_ssd_proj,
              gdn_conv_w, gdn_dt_bias, gdn_a_log, gdn_norm_w, w_gdn_proj, b_merge, w_out, ln2_w,
              moe_w_group, moe_b_group, moe_w_expert, moe_b_expert, moe_w_gate, moe_w_up, moe_w_down,
              final_norm_w):
    h = x
    for i in range(DEPTH):
        h = h + mixer_block(rms_norm(h, ln1_w[i]), w_in[i], ssd_conv_w[i], ssd_conv_b[i], ssd_dt_bias[i],
                            ssd_a_log[i], ssd_d[i], ssd_norm_w[i], w_ssd_proj[i], gdn_conv_w[i],
                            gdn_dt_bias[i], gdn_a_log[i], gdn_norm_w[i], w_gdn_proj[i], b_merge[i], w_out[i])
        h = h + hierarchical_moe(rms_norm(h, ln2_w[i]), moe_w_group[i], moe_b_group[i], moe_w_expert[i],
                                 moe_b_expert[i], moe_w_gate[i], moe_w_up[i], moe_w_down[i])
    return rms_norm(h, final_norm_w)


_drawn_inputs = setup_inputs


def setup_inputs(seed=0):
    import zlib

    import numpy as np

    out = dict(_drawn_inputs(seed))
    spreads = {}
    factors = {'ssd_d': 4.03,
     'ssd_norm_w': 4.252,
     'gdn_norm_w': 3.03,
     'b_merge': 4.628,
     'ln2_w': 2.788,
     'moe_b_group': 3.603,
     'moe_b_expert': 8.0,
     'final_norm_w': 2.802}
    for name, (base, spread) in spreads.items():
        noise = np.random.default_rng([zlib.crc32(name.encode()), seed]).standard_normal(out[name].shape)
        drawn = base * np.exp(spread * noise) if base else spread * noise
        out[name] = jnp.asarray(drawn.astype(out[name].dtype))
    for name, factor in factors.items():
        out[name] = (out[name] * factor).astype(out[name].dtype)
    return out
```

```python
from contextlib import ExitStack

import numpy as np

import concourse.bass as bass
from concourse import mybir

F32 = mybir.dt.float32
F32R = mybir.dt.float32r
I32 = mybir.dt.int32
U8 = mybir.dt.uint8
ALU = mybir.AluOpType
ACT = mybir.ActivationFunctionType
AX_X = mybir.AxisListType.X

P = 128
D = 1024
SEQ = 256
NT = SEQ // P
KC = D // P
EPS = 1e-6

SSD_INNER = 2048
SSD_HEADS = 32
SSD_HD = 64
SSD_GROUPS = 4
SSD_XBC = 3072
GDN_HEADS = 8
GDN_DIM = 1024
SMALL = SSD_HEADS + 2 * GDN_HEADS
DECAYS = SSD_HEADS + GDN_HEADS
LEVELS = 7

GROUPS = 4
EXPERTS = 4
FF = 512

PIECE = 2048
COLS = PIECE // KC

N_QKV, N_XBC, N_ZG, N_ZGDN = 12, 12, 16, 4
P_XBC = N_QKV
P_LOOP = P_XBC + N_XBC
P_ZGDN = P_LOOP + N_ZG
P_WGDN = P_ZGDN + N_ZGDN
P_WSSD = P_WGDN + 4
P_WOUT = P_WSSD + 8
N_MIX = P_WOUT + 4
N_CONV = N_QKV + N_XBC

MOE_PIECES = 6 * EXPERTS
RING = 4
MOE_RING = 8
MOE_HI = 6
SCATTER_0, SCATTER_1, TURN_SEL, NEXT_GROUP = 3, 6, 10, 22

C_ID, C_STRICT, C_CAUSAL, C_IOTA, C_END = 0, 128, 256, 640, 768
Q_CONV, Q_BMERGE, Q_LN1, Q_SSDN, Q_GDNN, Q_END = 0, 240, 256, 264, 280, 281
R_BIAS, R_ALOG, R_D, R_BG, R_BE, R_END = 0, 40, 80, 112, 116, 132


def moe_order():
    order = []
    for e in range(EXPERTS + 1):
        if e < EXPERTS:
            order += [("gate", e, 0), ("gate", e, 1), ("up", e, 0), ("up", e, 1)]
        if e >= 1:
            order += [("down", e - 1, 0), ("down", e - 1, 1)]
    return order


ORDER = moe_order()
TURN_H = {ORDER.index(("up", e, 1)) + 2: e for e in range(EXPERTS)}


def hybrid_layer(nc, w_mix, w_small, w_router, w_gate, w_up, w_down, x, consts, masks, params, rows, ln2,
                 final_w, out):
    ctx = ExitStack()
    with ctx:
        def sem(name):
            return ctx.enter_context(nc.semaphore(name))

        def sb(name, shape, dt=F32):
            return ctx.enter_context(nc.sbuf_tensor(name, shape, dt))

        landing = ExitStack()
        raw = landing.enter_context(nc.sbuf_tensor("raw", [P, RING, PIECE], F32))
        landing.close()
        rawlo = sb("rawlo", [P, RING, PIECE], F32R)
        whi = sb("whi", [P, 2, PIECE], F32R)
        cst = sb("cst", [P, C_END])
        lmask = sb("lmask", [P, 2, LEVELS, P], U8)
        prm = sb("prm", [P, Q_END])
        row = sb("row", [P, R_END])
        strict_r = sb("strict_r", [P, P], F32R)
        ones_r = sb("ones_r", [P, P], F32R)
        stat = sb("stat", [P, 8, 32])
        stat_i = sb("stat_i", [P, 32], I32)
        act_r = sb("act_r", [P, 2, KC, SEQ], F32R)

        mixer = ExitStack()
        cv = mixer.enter_context(nc.sbuf_tensor("cv", [P, 48, SEQ], F32))
        xy = mixer.enter_context(nc.sbuf_tensor("xy", [P, NT, SSD_INNER], F32))
        gates = mixer.enter_context(nc.sbuf_tensor("gates", [P, 16, SEQ], F32))
        mixer.close()
        landing = ExitStack()
        moe_raw = landing.enter_context(nc.sbuf_tensor("moe_raw", [P, 4, PIECE], F32))
        landing.close()
        moe_lo = sb("moe_lo", [P, 4, PIECE], F32R)
        moe_hi = sb("moe_hi", [P, 2, PIECE], F32R)
        xy_r = sb("xy_r", [P, NT, SSD_INNER], F32R)
        gates_r = sb("gates_r", [P, 2, PIECE], F32R)
        z = cv[:, 24:40, :].rearrange("p a b -> p (a b)").rearrange("p (t c) -> p t c", t=NT)
        o = cv[:, 40:48, :].rearrange("p a b -> p (a b)").rearrange("p (t c) -> p t c", t=NT)
        kqt = cv[:, 0:16, :].rearrange("p a b -> p (a b)").rearrange("p (h c) -> p h c", h=GDN_HEADS)
        sq = gates[:, :, :].rearrange("p a b -> p (a b)")
        qn = sq[:, 0:2048].rearrange("p (t c) -> p t c", t=NT)
        knorm1 = sq[:, 2048:3072]
        spare = cv[:, 16:24, :].rearrange("p a b -> p (a b)")
        kq_h = spare[:, 0:1024]
        inv = spare[:, 1024:1536]
        invt = spare[:, 1536:2048]
        mask_in = cv[:, 40:47, :].rearrange("p a b -> p (a b)")
        merged = spare.rearrange("p (a b) -> p a b", a=KC)
        xin = xy[:, 0, :].rearrange("p (t c) -> p t c", t=NT)
        xn = xy[:, 1, :].rearrange("p (t c) -> p t c", t=NT)
        ht = xy_r[:, 1, :].rearrange("p (b i f s) -> p b i f s", b=2, i=2, f=4)
        u = xin
        fin_out = xin

        front = ExitStack()

        def fsb(name, shape, dt=F32):
            return front.enter_context(nc.sbuf_tensor(name, shape, dt))

        ktok = fsb("ktok", [P, GDN_DIM])
        vtok = fsb("vtok", [P, NT, GDN_DIM])
        cbt = fsb("cbt", [P, SSD_GROUPS, 384])
        dtv = fsb("dtv", [P, NT, DECAYS])
        vdec = fsb("vdec", [P, NT, DECAYS])
        vdec_h = fsb("vdec_h", [P, NT, DECAYS], F32R)
        vdec_l = fsb("vdec_l", [P, NT, DECAYS])
        beta = fsb("beta", [P, NT, GDN_HEADS])
        nbeta = fsb("nbeta", [P, NT, GDN_HEADS])
        egc = fsb("egc", [P, NT, GDN_HEADS])
        negc = fsb("negc", [P, GDN_HEADS])
        kdec = fsb("kdec", [P, GDN_HEADS])
        small_sb = fsb("small_sb", [P, NT, SMALL])
        tmp = fsb("tmp", [P, 6, NT, DECAYS])
        early = ExitStack()

        def esb(name, shape, dt=F32):
            return early.enter_context(nc.sbuf_tensor(name, shape, dt))

        cacc = esb("cacc", [P, 2, 2, SEQ])
        sml = esb("sml", [P, KC * SMALL])
        sml_h = esb("sml_h", [P, KC * SMALL], F32R)
        sml_l = esb("sml_l", [P, KC * SMALL], F32R)
        early.close()
        ssdrhs = fsb("ssdrhs", [P, 2, 2, 384], F32R)
        ldec = fsb("ldec", [P, 2, 384])
        gdnrhs = fsb("gdnrhs", [P, 2, 512], F32R)
        gdec = fsb("gdec", [P, 512])
        gdecm = fsb("gdecm", [P, 512])
        nmat = fsb("nmat", [P, 512])
        pmat = fsb("pmat", [P, 512])
        aqk = fsb("aqk", [P, 512])
        kd = fsb("kd", [P, 2, P])
        vnew = fsb("vnew", [P, 2, 2, P])
        s1 = fsb("s1", [P, 256])
        resid = fsb("resid", [P, 2, P])
        qs = fsb("qs", [P, 256])
        sink = fsb("sink", [P, 16])
        xd = fsb("xd", [P, NT, 4, SSD_HD])
        front.close()

        hres = sb("hres", [P, NT, D])
        osq = hres[:, :, :].rearrange("p t c -> p (t c)")
        back = ExitStack()

        def bsb(name, shape, dt=F32):
            return back.enter_context(nc.sbuf_tensor(name, shape, dt))

        zg = bsb("zg", [P, NT, GDN_DIM])
        yt = bsb("yt", [P, 2, 16, SEQ], F32R)
        mtmp = bsb("mtmp", [P, 2, SEQ])
        back.close()

        xg = sb("xg", [P, 2, KC, P], F32R)
        hs = sb("hs", [P, 2048])
        ut = hs[:, :].rearrange("p (k s) -> p k s", k=KC)
        hbuf = hs[:, 0:1024].rearrange("p (b f) -> p b f", b=2)
        sgate = hs[:, 1024:1536]
        ysp = sb("ysp", [P, 2, D], F32R)
        sel = sb("sel", [P, NT, P])
        selt = sb("selt", [P, NT, P], F32R)
        cslot = sb("cslot", [P, EXPERTS])
        ln2b = sb("ln2b", [P, D])
        finb = sb("finb", [P, D])
        wr = sb("wr", [P, KC * 20])
        rt = sb("rt", [P, 24, NT, 4])
        rl = sb("rl", [P, NT, 20])
        re = sb("re", [P, NT, 16])
        qsl = sb("qsl", [P, NT, 8])
        cw = sb("cw", [P, NT, EXPERTS])
        rinfo = sb("rinfo", [P, 8])
        rint = sb("rint", [P, 2], I32)
        mring = [raw[:, j, :] for j in range(RING)]
        mring += [moe_raw[:, j, :] for j in range(4)]
        los = [rawlo[:, j, :] for j in range(RING)] + [moe_lo[:, j, :] for j in range(4)]
        his = [t[:, j, :] for t in (whi, gates_r, moe_hi) for j in range(2)]
        assert len(mring) == MOE_RING and len(his) == MOE_HI

        ps = ctx.enter_context(nc.psum_tensor("ps", [P, 8, 512], F32))

        ident = cst[:, C_ID:C_ID + P]
        strict = cst[:, C_STRICT:C_STRICT + P]
        causal = cst[:, C_CAUSAL:C_CAUSAL + P]
        ones = cst[:, C_CAUSAL + P:C_CAUSAL + 2 * P]
        causal2 = cst[:, C_CAUSAL:C_CAUSAL + 256]
        causal3 = cst[:, C_CAUSAL:C_CAUSAL + 384]
        iota = cst[:, C_IOTA:C_IOTA + P]

        s_x, s_cst, s_out = sem("s_x"), sem("s_cst"), sem("s_out")
        s_sml, s_xres, s_moep = sem("s_sml"), sem("s_xres"), sem("s_moep")
        landed = [sem(f"landed{j}") for j in range(RING)]
        mlanded = [sem(f"mlanded{j}") for j in range(MOE_RING)]
        hi_done, lo_done, piece_mm = sem("hi_done"), sem("lo_done"), sem("piece_mm")
        acc_free = sem("acc_free")
        dve_step = sem("dve_step")
        ss_in, r_in, xn_done, xt_mm, xt_hi = (sem(n) for n in ("ss_in", "r_in", "xn_done", "xt_mm", "xt_hi"))
        xt_lo, cst_r, sml_hi, sml_lo, sml_mm = (sem(n) for n in ("xt_lo", "cst_r", "sml_hi", "sml_lo", "sml_mm"))
        tap3_done, tap_step, silu_done = sem("tap3_done"), sem("tap_step"), sem("silu_done")
        sq_done, ss_mm, norm_done = sem("sq_done"), sem("ss_mm"), sem("norm_done")
        fill_mm, evac_a, evac_d = sem("fill_mm"), sem("evac_a"), sem("evac_d")
        dec_in, dec_exp, dec_v, dec_mm, dec_tab, tab_done = (
            sem(n) for n in ("dec_in", "dec_exp", "dec_v", "dec_mm", "dec_tab", "tab_done"))
        g_staged, g_rhs, g_kq, g_seg, g_exp, g_mask, g_nt, g_aqk, g_kd = (
            sem(n) for n in ("g_staged", "g_rhs", "g_kq", "g_seg", "g_exp", "g_mask", "g_nt", "g_aqk", "g_kd"))
        g_eye, g_ntt, g_x, g_y, g_p, g_ps, g_xp, g_yp = (
            sem(n) for n in ("g_eye", "g_ntt", "g_x", "g_y", "g_p", "g_ps", "g_xp", "g_yp"))
        g_solve, g_vn, g_state, g_scopy, g_ocopy, g_ks, g_qs, g_r, g_o1, g_oadd = (
            sem(n) for n in ("g_solve", "g_vn", "g_state", "g_scopy", "g_ocopy", "g_ks", "g_qs", "g_r", "g_o1",
                             "g_oadd"))
        m_rhs, m_seg, m_exp, m_gl, m_y, m_xd, m_ydone = (
            sem(n) for n in ("m_rhs", "m_seg", "m_exp", "m_gl", "m_y", "m_xd", "m_ydone"))
        b_osq, b_red, b_o, b_z, b_yz, b_yss, b_yr, b_ys, b_gate, b_zg = (
            sem(n) for n in ("b_osq", "b_red", "b_o", "b_z", "b_yz", "b_yss", "b_yr", "b_ys", "b_gate", "b_zg"))
        bt_mm, bt_hi, bt_lo, b_m, b_mhi, b_mlo, b_h = (
            sem(n) for n in ("bt_mm", "bt_hi", "bt_lo", "b_m", "b_mhi", "b_mlo", "b_h"))
        b_mt = sem("b_mt")
        n_ss, n_u, n_ut, n_utc, n_log, n_lg, n_exp, n_oh, n_cnt, n_route = (
            sem(n) for n in ("n_ss", "n_u", "n_ut", "n_utc", "n_log", "n_lg", "n_exp", "n_oh", "n_cnt",
                             "n_route"))
        e_sel, e_gath, e_xhi, e_xlo, e_silu, e_h, e_ht, e_hthi, e_htlo = (
            sem(n) for n in ("e_sel", "e_gath", "e_xhi", "e_xlo", "e_silu", "e_h", "e_ht", "e_hthi", "e_htlo"))
        e_turn, e_back, e_zero = sem("e_turn"), sem("e_back"), sem("e_zero")
        e_yhi, e_ylo, e_scat, e_add = (sem(n) for n in ("e_yhi", "e_ylo", "e_scat", "e_add"))
        f_ss, f_out = sem("f_ss"), sem("f_out")

        fills = [("v", i, "a") for i in range(4)] + [("x", i, "a") for i in range(8)]
        fills += [("cb", i, "d") for i in range(4)]
        fills += [("k", i, "d") for i in range(4)] + [("q", i, "d") for i in range(4)]
        fills += [("kqt", i, "a") for i in range(8)]
        fill_no, evac_no, seen = {}, [], {"a": 0, "d": 0}
        for f, (what, i, who) in enumerate(fills):
            fill_no[what, i] = f
            seen[who] += 1
            evac_no.append((who, seen[who]))

        def wait_evac(eng, f):
            who, n = evac_no[f]
            eng.wait_ge(evac_a if who == "a" else evac_d, n)

        def bank(f):
            return ps[:, 2 + f % 6, :]

        def f32(ap):
            return ap.bitcast(F32)

        def two(ap):
            return ap.rearrange("p (a b) -> p a b", a=2)

        def four(ap):
            return ap.rearrange("p (a b) -> p a b", a=4)

        block = ctx.enter_context(nc.Block())

        @block.sync
        def _(sp):
            sp.dma_start(xin, x.rearrange("b (t p) c -> p (b t) c", p=P)).then_inc(s_x, 16)
            for p in range(RING):
                sp.dma_start(raw[:, p, :], w_mix[p]).then_inc(landed[p], 16)
            with sp.Fori(1, N_MIX // RING) as q:
                for j in range(RING):
                    sp.wait_ge(piece_mm, q * RING + (j - RING + 1))
                    sp.dma_start(raw[:, j, :], w_mix[bass.ds(q * RING + j, 1)].rearrange("a p c -> p (a c)"))\
                        .then_inc(landed[j], 16)

            def moe_piece(g, it, n, first):
                kind, e, half = ORDER[n]
                slot = n % MOE_RING
                if first and n < MOE_RING:
                    if slot < RING:
                        sp.wait_ge(piece_mm, N_MIX - RING + 1 + slot)
                    elif slot == RING:
                        sp.wait_ge(b_mhi, 1)
                        sp.wait_ge(b_mlo, 1)
                else:
                    sp.wait_ge(piece_mm, it * MOE_PIECES + (N_MIX + n - MOE_RING + 1))
                w = {"gate": w_gate, "up": w_up, "down": w_down}[kind]
                src = w[bass.ds(g * EXPERTS + e, 1), :, half * PIECE:(half + 1) * PIECE]
                sp.dma_start(mring[slot], src.rearrange("a p c -> p (a c)")).then_inc(mlanded[slot], 16)

            for n in range(MOE_PIECES):
                moe_piece(0, 0, n, True)
            with sp.Fori(1, GROUPS) as g:
                for n in range(MOE_PIECES):
                    moe_piece(g, g, n, False)
            sp.wait_ge(n_route, 1)
            again = sp.value_load(rint[0:1, 0:1], min_val=GROUPS, max_val=GROUPS + 1)
            big = sp.value_load(rint[0:1, 1:2], min_val=0, max_val=GROUPS - 1)
            with sp.If(again > GROUPS):
                for n in range(MOE_PIECES):
                    moe_piece(big, GROUPS, n, False)
            sp.wait_ge(f_out, NT)
            sp.dma_start(out.rearrange("b (t p) c -> p (b t) c", p=P), fin_out).then_inc(s_out, 16)
            sp.wait_ge(s_out, 16)

        @block.scalar
        def _(act):
            act.dma_start(cst[:, :], consts).then_inc(s_cst, 16)
            act.dma_start(mask_in, masks).then_inc(s_cst, 16)
            act.dma_start(prm[:, :], params).then_inc(s_cst, 16)
            act.dma_start(row[:, :], rows.partition_broadcast(P)).then_inc(s_cst, 16)
            act.dma_start(sml[:, :], w_small).then_inc(s_sml, 16)

            def hi(q, j, slots=2):
                act.wait_ge(landed[j], q * 16 + 16)
                if not (isinstance(q, int) and q == 0):
                    act.wait_ge(piece_mm, q * RING + (j - slots + 1))
                act.copy(his[j % slots], raw[:, j, :]).then_inc(hi_done, 1)

            act.wait_ge(s_x, 16)
            for t in range(NT):
                act.activation(xn[:, t, :], xin[:, t, :], ACT.Square,
                               accum_out=stat[:, 0, t:t + 1]).then_inc(ss_in, 1)
            act.wait_ge(r_in, 1)
            act.wait_ge(ss_in, NT)
            for t in range(NT):
                act.activation(xn[:, t, :], xin[:, t, :], ACT.Copy,
                               scale=stat[:, 1, t:t + 1]).then_inc(xn_done, 1)
            act.wait_ge(s_sml, 16)
            act.copy(sml_h[:, :], sml[:, :]).then_inc(sml_hi, 1)
            hi(0, 0)
            hi(0, 1)
            act.wait_ge(s_cst, 64)
            for k in range(KC):
                act.wait_ge(xt_mm, k // 2 + 1)
                act.activation(act_r[:, 0, k, :], ps[:, 2 + k // 2, (k % 2) * SEQ:(k % 2 + 1) * SEQ], ACT.Copy,
                               scale=prm[:, Q_LN1 + k:Q_LN1 + k + 1]).then_inc(xt_hi, 1)

            def tap3(p, j):
                act.wait_ge(piece_mm, p + 1)
                if isinstance(p, int) and p < 2:
                    pass
                else:
                    act.wait_ge(silu_done, p - 1)
                for m in range(2):
                    c = Q_CONV + m * 5
                    ins = act.activation(cacc[:, j % 2, m, :], ps[:, j, m * SEQ:(m + 1) * SEQ], ACT.Identity,
                                         bias=prm[:, bass.ds(p * 10 + (c + 4), 1)],
                                         scale=prm[:, bass.ds(p * 10 + (c + 3), 1)])
                ins.then_inc(tap3_done, 1)

            def silu(p, j):
                act.wait_ge(tap_step, p * 6 + 6)
                act.activation(cv[:, bass.ds(p * 2, 2), :], cacc[:, j % 2, :, :], ACT.Silu).then_inc(silu_done, 1)

            act.wait_ge(cst_r, 3)
            for p in range(RING):
                hi((p + 2) // RING, (p + 2) % RING, RING)
                tap3(p, p)
                if p >= 1:
                    silu(p - 1, p - 1)
            with act.Fori(1, N_CONV // RING) as q:
                for j in range(RING):
                    hi(q + (j + 2) // RING, (j + 2) % RING, RING)
                    tap3(q * RING + j, j)
                    silu(q * RING + (j - 1), j - 1)
            silu(N_CONV - 1, 1)

            act.wait_ge(silu_done, N_CONV)
            for i in range(4):
                act.activation(sq[:, i * 1024:(i + 1) * 1024],
                               cv[:, 4 * i:4 * i + 4, :].rearrange("p a b -> p (a b)"),
                               ACT.Square).then_inc(sq_done, 1)
            for what, dst in (("v", vtok), ("x", xy)):
                for i in range(4 if what == "v" else 8):
                    f = fill_no[what, i]
                    act.wait_ge(fill_mm, f + 1)
                    act.copy(dst[:, i % NT, (i // NT) * 512:(i // NT + 1) * 512], bank(f)).then_inc(evac_a, 1)
            act.wait_ge(dec_in, 1)
            act.activation(tmp[:, 2, :, :], tmp[:, 1, :, :], ACT.Exp).then_inc(dec_exp, 1)
            act.activation(tmp[:, 4, 0, :], row[:, R_ALOG:R_ALOG + DECAYS], ACT.Exp).then_inc(dec_exp, 1)
            act.activation(beta[:, :, :], nbeta[:, :, :], ACT.Exp).then_inc(dec_exp, 1)
            act.wait_ge(dec_mm, 1)
            act.activation(egc[:, :, :], ps[:, 0, 0:16].rearrange("p (t h) -> p t h", t=NT),
                           ACT.Exp).then_inc(dec_tab, 1)
            act.activation(kdec[:, :], ps[:, 0, 16:24], ACT.Exp).then_inc(dec_tab, 1)
            for i in range(GDN_HEADS):
                f = fill_no["kqt", i]
                act.wait_ge(fill_mm, f + 1)
                act.copy(kqt[:, i, :], bank(f)).then_inc(evac_a, 1)

            with act.Fori(0, GDN_HEADS // 2) as it:
                def take(j):
                    act.wait_ge(piece_mm, it * 4 + (P_LOOP + j + 1))
                    if j % 2 == 0:
                        act.copy(z[:, :, bass.ds(it * 512 + (j // 2) * COLS, COLS)],
                                 two(ps[:, 0, :])).then_inc(acc_free, 1)
                    else:
                        for m in range(2):
                            ins = act.activation(
                                gates[:, bass.ds(it * 4 + ((j // 2) * 2 + m), 1), :].rearrange("p a b -> p (a b)"),
                                ps[:, 1, m * SEQ:(m + 1) * SEQ], ACT.Identity,
                                bias=prm[:, bass.ds(it * 4 + (Q_BMERGE + (j // 2) * 2 + m), 1)])
                        ins.then_inc(acc_free, 1)

                def decay_exp(k):
                    act.wait_ge(m_seg, it * 8 + (k + 1))
                    if k >= 2:
                        act.wait_ge(m_y, it * 8 + (k - 1))
                    act.activation(ldec[:, k % 2, :], ps[:, 5 + k % 2, 0:384], ACT.Exp).then_inc(m_exp, 1)

                def pcopy(l):
                    act.wait_ge(g_p, it * 6 + l)
                    act.copy(pmat[:, :], ps[:, 2, :]).then_inc(g_ps, 1)

                def vscale(c):
                    act.wait_ge(g_solve, it * 2 + (c + 1))
                    for h in range(2):
                        ins = act.activation(vnew[:, c, h, :], ps[:, 2, h * P:(h + 1) * P], ACT.Copy,
                                             scale=beta[:, c, bass.ds(it * 2 + h, 1)])
                    ins.then_inc(g_vn, 1)

                for h in range(2):
                    ins = act.activation(kd[:, h, :], ktok[:, bass.ds(it * 256 + h * P, P)], ACT.Copy,
                                         scale=kdec[:, bass.ds(it * 2 + h, 1)])
                ins.then_inc(g_kd, 1)
                act.wait_ge(g_seg, it + 1)
                act.activation(gdec[:, :], ps[:, 4, :], ACT.Exp).then_inc(g_exp, 1)
                decay_exp(0)
                decay_exp(1)
                pcopy(1)
                decay_exp(2)
                decay_exp(3)
                pcopy(2)
                decay_exp(4)
                decay_exp(5)
                take(0)
                hi(it + P_LOOP // RING, 2)
                pcopy(3)
                decay_exp(6)
                decay_exp(7)
                pcopy(4)
                take(1)
                hi(it + P_LOOP // RING, 3)
                pcopy(5)
                pcopy(6)
                vscale(0)
                act.wait_ge(g_state, it + 1)
                act.copy(s1[:, :], ps[:, 3, 0:256]).then_inc(g_scopy, 1)
                take(2)
                hi(it + (P_LOOP // RING + 1), 0)
                act.wait_ge(g_ks, it + 1)
                for h in range(2):
                    ins = act.activation(qs[:, h * P:(h + 1) * P], ps[:, 3, h * P:(h + 1) * P], ACT.Copy,
                                         scale=egc[:, 1, bass.ds(it * 2 + h, 1)])
                ins.then_inc(g_qs, 1)
                vscale(1)
                take(3)
                hi(it + (P_LOOP // RING + 1), 1)

            act.wait_ge(g_oadd, GDN_HEADS // 2)
            act.activation(osq, o.rearrange("p t c -> p (t c)"), ACT.Square).then_inc(b_osq, 1)
            for i in range(N_ZGDN):
                p = P_ZGDN + i
                act.wait_ge(piece_mm, p + 1)
                act.activation(zg[:, :, i * COLS:(i + 1) * COLS], two(ps[:, p % 2, :]),
                               ACT.Silu).then_inc(acc_free, 1)
                hi(*divmod(p + 2, RING))
                act.activation(z[:, i // 2, (i % 2) * 1024:(i % 2 + 1) * 1024],
                               z[:, i // 2, (i % 2) * 1024:(i % 2 + 1) * 1024], ACT.Silu).then_inc(b_z, 1)
            for i in range(4):
                gi = gates[:, 4 * i:4 * i + 4, :].rearrange("p a b -> p (a b)")
                act.activation(gi, gi, ACT.Tanh, scale=0.5).then_inc(b_gate, 1)
            act.wait_ge(b_red, 1)
            act.dma_start(hres[:, :, :], x.rearrange("b (t p) c -> p (b t) c", p=P)).then_inc(s_xres, 16)
            for t in range(NT):
                act.wait_ge(b_yz, t + 1)
                act.activation(z[:, t, :], xy[:, t, :], ACT.Square, accum_out=stat[:, 0, t:t + 1]).then_inc(b_yss, 1)

            def back_hi(f):
                act.wait_ge(bt_mm, f + 1)
                if f < 4:
                    act.activation(act_r[:, 0, 2 * f:2 * f + 2, :], two(ps[:, 4 + f % 4, :]), ACT.Copy,
                                   scale=prm[:, Q_GDNN:Q_GDNN + 1]).then_inc(bt_hi, 1)
                else:
                    for m in range(2):
                        a = 2 * (f - 4) + m
                        ins = act.activation(yt[:, 0, a, :], ps[:, 4 + f % 4, m * SEQ:(m + 1) * SEQ], ACT.Copy,
                                             scale=prm[:, Q_SSDN + a:Q_SSDN + a + 1])
                    ins.then_inc(bt_hi, 1)

            for f in range(4):
                back_hi(f)
            act.wait_ge(b_yr, 1)
            act.wait_ge(b_yss, NT)
            for t in range(NT):
                act.activation(xy[:, t, :], xy[:, t, :], ACT.Copy, scale=stat[:, 1, t:t + 1]).then_inc(b_ys, 1)
            hi(*divmod(P_WGDN + 2, RING))
            for f in range(4, 8):
                back_hi(f)
            hi(*divmod(P_WGDN + 3, RING))
            for f in range(8, 12):
                back_hi(f)
            for p in range(P_WGDN + 4, N_MIX):
                hi(*divmod(p, RING))
                if p == P_WOUT + 1:
                    act.wait_ge(b_m, 8)
                    act.copy(act_r[:, 0, :, :], merged).then_inc(b_mhi, 1)

            act.dma_start(ln2b[:, :], ln2.partition_broadcast(P)).then_inc(s_moep, 16)
            act.dma_start(finb[:, :], final_w.partition_broadcast(P)).then_inc(s_moep, 16)
            act.dma_start(wr[:, :], w_router).then_inc(s_moep, 16)
            act.wait_ge(b_h, 4)
            for t in range(NT):
                act.activation(u[:, t, :], hres[:, t, :], ACT.Square, accum_out=stat[:, 0, t:t + 1]).then_inc(n_ss, 1)
            for f in range(4):
                act.wait_ge(n_ut, f + 1)
                act.copy(hs[:, f * 512:(f + 1) * 512], ps[:, 4 + f, :]).then_inc(n_utc, 1)
            act.wait_ge(n_lg, 1)
            act.activation(rt[:, 4, :, :], rt[:, 3, :, :], ACT.Exp).then_inc(n_exp, 1)
            act.wait_ge(n_lg, 2)
            act.activation(rt[:, 16, :, 0:1], rt[:, 15, :, 0:1], ACT.Exp).then_inc(n_exp, 1)
            act.wait_ge(n_route, 1)
            runs = act.value_load(rint[0:1, 0:1], min_val=GROUPS, max_val=GROUPS + 1)

            def x_high(it):
                act.wait_ge(e_gath, it + 1)
                act.copy(xg[:, 0, :, :].rearrange("p k s -> p (k s)"),
                         ps[:, 0:2, :].rearrange("p a b -> p (a b)")).then_inc(e_xhi, 1)

            def y_high(it):
                act.wait_ge(e_zero, 2)
                act.wait_ge(piece_mm, it * MOE_PIECES + N_MIX)
                act.copy(ysp[:, 0, :], ps[:, 4:6, :].rearrange("p a b -> p (a b)")).then_inc(e_yhi, 1)

            x_high(0)
            with act.Fori(0, runs) as it:
                def mhi(n):
                    slot = n % MOE_RING
                    act.wait_ge(mlanded[slot], it * (16 * MOE_PIECES // MOE_RING) + 16 * (n // MOE_RING + 1))
                    act.wait_ge(piece_mm, it * MOE_PIECES + (N_MIX + n - MOE_HI + 1))
                    act.copy(his[n % MOE_HI], mring[slot]).then_inc(hi_done, 1)

                mhi(0)
                mhi(1)
                y_high(it)
                mhi(2)
                mhi(3)
                for n, (kind, e, half) in enumerate(ORDER):
                    if n + 4 < MOE_PIECES:
                        mhi(n + 4)
                    if (kind, half) == ("gate", 1):
                        act.wait_ge(piece_mm, it * MOE_PIECES + (N_MIX + n + 1))
                        if e >= 1:
                            act.wait_ge(e_h, it * EXPERTS + e)
                        act.activation(sgate, ps[:, 2 * (e % 2), :], ACT.Silu).then_inc(e_silu, 1)
                    if n + 1 in TURN_H:
                        d = TURN_H[n + 1]
                        act.wait_ge(e_ht, it * EXPERTS + (d + 1))
                        act.copy(ht[:, d % 2, 0, :, :].rearrange("p a b -> p (a b)"), ps[:, 6, :]).then_inc(e_hthi, 1)
                    if n + 1 == TURN_SEL:
                        act.wait_ge(e_turn, it + 1)
                        act.copy(selt[:, :, :].rearrange("p t s -> p (t s)"), ps[:, 7, P:3 * P]).then_inc(e_back, 1)
                    if n + 1 == NEXT_GROUP:
                        x_high(it + 1)
            y_high(runs)

            act.wait_ge(e_add, runs * 2 + 2)
            for t in range(NT):
                act.activation(u[:, t, :], hres[:, t, :], ACT.Square, accum_out=stat[:, 0, t:t + 1]).then_inc(f_ss, 1)

        @block.vector
        def _(dve):
            chain = [0]

            def link(ins):
                chain[0] += 1
                ins.then_inc(dve_step, 1)
                dve.wait_ge(dve_step, chain[0])

            def rsqrt(n, scale, last_sem):
                v, y, t1, t2 = (stat[:, i, 0:n] for i in (2, 1, 3, 4))
                link(dve.tensor_scalar(v, stat[:, 0, 0:n], scale, EPS, ALU.mult, ALU.add))
                link(dve.tensor_scalar(stat_i[:, 0:n], v.bitcast(I32), 1, None, ALU.logical_shift_right))
                link(dve.tensor_scalar(y.bitcast(I32), stat_i[:, 0:n], -1.0, 1597463007.0, ALU.mult, ALU.add))
                for i in range(4):
                    link(dve.scalar_tensor_tensor(t1, y, -0.5, y, ALU.mult, ALU.mult))
                    link(dve.tensor_tensor(t2, t1, v, ALU.mult))
                    ins = dve.scalar_tensor_tensor(y, t2, 1.5, y, ALU.add, ALU.mult)
                    if i < 3 or last_sem is None:
                        link(ins)
                    else:
                        ins.then_inc(last_sem, 1)

            def lo(q, j, slots=2):
                dve.wait_ge(hi_done, q * RING + (j + 1))
                dve.tensor_tensor(los[j], raw[:, j, :], f32(his[j % slots]),
                                  ALU.subtract).then_inc(lo_done, 1)

            dve.wait_ge(ss_in, NT)
            rsqrt(NT, 1.0 / D, r_in)
            dve.wait_ge(s_cst, 64)
            dve.tensor_copy(strict_r[:, :], strict).then_inc(cst_r, 1)
            dve.tensor_copy(ones_r[:, :], ones).then_inc(cst_r, 1)
            dve.tensor_copy(lmask[:, :, :, :].rearrange("p a l c -> p (a l c)"),
                            mask_in).then_inc(cst_r, 1)
            dve.wait_ge(sml_hi, 1)
            dve.tensor_tensor(sml_l[:, :], sml[:, :], f32(sml_h[:, :]), ALU.subtract).then_inc(sml_lo, 1)
            lo(0, 0)
            lo(0, 1)
            for k in range(KC):
                dve.wait_ge(xt_hi, k // 2 * 2 + 2)
                dve.scalar_tensor_tensor(act_r[:, 1, k, :], ps[:, 2 + k // 2, (k % 2) * SEQ:(k % 2 + 1) * SEQ],
                                         prm[:, Q_LN1 + k:Q_LN1 + k + 1], f32(act_r[:, 0, k, :]),
                                         ALU.mult, ALU.subtract).then_inc(xt_lo, 1)
            dve.wait_ge(sml_mm, 1)
            dve.tensor_copy(small_sb[:, :, :],
                            ps[:, 6, 0:NT * SMALL].rearrange("p (t c) -> p t c", t=NT)).then_inc(sml_lo, 1)

            def taps(p, j):
                dve.wait_ge(tap3_done, p + 1)
                for k in (1, 2, 3):
                    for m in range(2):
                        if k >= 2:
                            dve.wait_ge(tap_step, p * 6 + (2 * (k - 2) + m + 1))
                        acc = cacc[:, j % 2, m, k:SEQ]
                        dve.scalar_tensor_tensor(acc, ps[:, j, m * SEQ:(m + 1) * SEQ - k],
                                                 prm[:, bass.ds(p * 10 + (Q_CONV + m * 5 + 3 - k), 1)], acc,
                                                 ALU.mult, ALU.add).then_inc(tap_step, 1)

            with dve.Fori(0, N_CONV // RING) as q:
                for j in range(RING):
                    lo(q + (j + 2) // RING, (j + 2) % RING, RING)
                    taps(q * RING + j, j)
            dve.wait_ge(tap_step, 6 * N_CONV)
            dve.memset(stat[:, 7, 0:1], 0.0).then_inc(acc_free, 2)

            pre, na, e, s2, acc, s = (tmp[:, i, :, :] for i in (0, 1, 2, 3, 4, 5))
            dve.wait_ge(sml_lo, 2)
            link(dve.tensor_tensor(pre, small_sb[:, :, 0:DECAYS],
                                   row[:, R_BIAS:R_BIAS + DECAYS].unsqueeze(1).broadcast_to([P, NT, DECAYS]), ALU.add))
            link(dve.tensor_scalar(na, pre, -1.0, None, ALU.mult))
            link(dve.tensor_tensor(na, na, pre, ALU.min))
            dve.tensor_scalar(nbeta[:, :, :], small_sb[:, :, DECAYS:SMALL], -1.0, 80.0,
                              ALU.mult, ALU.min).then_inc(dec_in, 1)
            dve.wait_ge(dec_exp, 3)
            a_neg = stat[:, 5:7, :].rearrange("p a b -> p (a b)")[:, 0:DECAYS]
            link(dve.tensor_scalar(a_neg, tmp[:, 4, 0, :], -1.0, None, ALU.mult))
            link(dve.tensor_scalar(acc, e, 2.0, None, ALU.add))
            link(dve.reciprocal(s2, acc))
            link(dve.tensor_tensor(s, e, s2, ALU.mult))
            link(dve.tensor_tensor(s2, s, s, ALU.mult))
            link(dve.tensor_scalar(acc, s2, 1.0 / 15, None, ALU.mult))
            for c in (13, 11, 9, 7, 5, 3):
                link(dve.scalar_tensor_tensor(acc, acc, 1.0 / c, s2, ALU.add, ALU.mult))
            link(dve.scalar_tensor_tensor(acc, acc, 1.0, s, ALU.add, ALU.mult))
            link(dve.tensor_scalar(na, pre, 0.0, None, ALU.max))
            link(dve.scalar_tensor_tensor(dtv[:, :, :], acc, 2.0, na, ALU.mult, ALU.add))
            link(dve.tensor_tensor(vdec[:, :, :], dtv[:, :, :],
                                   a_neg.unsqueeze(1).broadcast_to([P, NT, DECAYS]), ALU.mult))
            link(dve.tensor_copy(vdec_h[:, :, :], vdec[:, :, :]))
            dve.tensor_tensor(vdec_l[:, :, :], vdec[:, :, :], f32(vdec_h[:, :, :]), ALU.subtract).then_inc(dec_v, 1)
            link(dve.tensor_scalar(beta[:, :, :], beta[:, :, :], 1.0, None, ALU.add))
            link(dve.reciprocal(beta[:, :, :], beta[:, :, :]))
            dve.tensor_scalar(nbeta[:, :, :], beta[:, :, :], -1.0, None, ALU.mult).then_inc(tab_done, 1)
            dve.wait_ge(dec_tab, 2)
            dve.tensor_scalar(negc[:, :], egc[:, 1, :], -1.0, None, ALU.mult).then_inc(tab_done, 1)

            for i in range(SSD_GROUPS):
                f = fill_no["cb", i]
                dve.wait_ge(fill_mm, f + 1)
                dve.tensor_tensor(cbt[:, i, :], bank(f)[:, 0:384], causal3, ALU.mult).then_inc(evac_d, 1)
            dve.wait_ge(ss_mm, 1)
            link(dve.tensor_copy(stat[:, 0, :], ps[:, 1, 0:32]))
            rsqrt(32, 1.0, None)
            rq = stat[:, 1, :].rearrange("p (t h) -> p t h", t=NT)
            link(dve.tensor_scalar(rq[:, :, 0:8], rq[:, :, 0:8], float(P) ** -0.5, None, ALU.mult))
            for what, off in (("k", 8), ("q", 0)):
                for i in range(4):
                    f = fill_no[what, i]
                    t, b = i % NT, i // NT
                    dst = qn[:, t, :] if what == "q" else (ktok[:, :] if t == 0 else knorm1)
                    dve.wait_ge(fill_mm, f + 1)
                    dve.tensor_tensor(
                        four(dst[:, b * 512:(b + 1) * 512]), four(bank(f)),
                        rq[:, t, off + 4 * b:off + 4 * b + 4].unsqueeze(2).broadcast_to([P, 4, P]),
                        ALU.mult).then_inc(evac_d, 1)

            with dve.Fori(0, GDN_HEADS // 2) as it:
                def scores(k):
                    dve.wait_ge(m_exp, it * 8 + (k + 1))
                    for t, (a, b) in enumerate(((0, 256), (256, 384))):
                        ins = dve.scalar_tensor_tensor(
                            ldec[:, k % 2, a:b], cbt[:, bass.ds(it, 1), a:b].rearrange("p a b -> p (a b)"),
                            dtv[:, t, bass.ds(it * 8 + k, 1)], ldec[:, k % 2, a:b], ALU.mult, ALU.mult)
                    ins.then_inc(m_gl, 1)

                def merge_level(l):
                    if l < 6:
                        dve.wait_ge(g_xp, it * 5 + l)
                        dve.wait_ge(g_x, it * 6 + l)
                        dve.memset(sink[:, 2 * l:2 * l + 1], 0.0)
                        dve.copy_predicated(four(inv), lmask[:, 0, l, :].unsqueeze(1).broadcast_to([P, 4, P]),
                                            four(ps[:, 3, :])).then_inc(g_x, 1)
                    dve.wait_ge(g_yp, it * 6 + l)
                    dve.wait_ge(g_y, it * 7 + l)
                    dve.memset(sink[:, 2 * l + 1:2 * l + 2], 0.0)
                    dve.copy_predicated(four(invt), lmask[:, 1, l, :].unsqueeze(1).broadcast_to([P, 4, P]),
                                        four(ps[:, 4, :])).then_inc(g_y, 1)

                def y_add(k):
                    dve.wait_ge(m_y, it * 8 + (4 * k + 4))
                    dve.wait_ge(m_xd, it * 2 + (k + 1))
                    dve.tensor_tensor(xy[:, :, bass.ds(it * 512 + k * 256, 256)], two(ps[:, 7, :]),
                                      xd[:, :, :, :].rearrange("p t h d -> p t (h d)"), ALU.add).then_inc(m_ydone, 1)

                dve.wait_ge(g_kq, it + 1)
                dve.wait_ge(g_exp, it + 1)
                for h in range(2):
                    for c in range(NT):
                        n = 2 * h + c
                        ins = dve.scalar_tensor_tensor(
                            nmat[:, n * P:(n + 1) * P], ps[:, 2 + h, c * 256:c * 256 + P],
                            nbeta[:, c, bass.ds(it * 2 + h, 1)], gdec[:, n * P:(n + 1) * P], ALU.mult, ALU.mult)
                ins.then_inc(g_nt, 1)
                scores(0)
                scores(1)
                dve.wait_ge(g_mask, it + 1)
                for h in range(2):
                    ins = dve.tensor_tensor(two(aqk[:, h * 256:(h + 1) * 256]), two(ps[:, 2 + h, :])[:, :, P:2 * P],
                                            two(gdecm[:, h * 256:(h + 1) * 256]), ALU.mult)
                ins.then_inc(g_aqk, 1)
                dve.wait_ge(g_eye, it * 2 + 2)
                dve.wait_ge(g_ntt, it + 1)
                dve.wait_ge(g_nt, it + 1)
                dve.memset(sink[:, 0:1], 0.0)
                dve.copy_predicated(four(inv), lmask[:, 0, 0, :].unsqueeze(1).broadcast_to([P, 4, P]),
                                    four(ps[:, 4, :])).then_inc(g_x, 1)
                dve.copy_predicated(four(invt), lmask[:, 1, 0, :].unsqueeze(1).broadcast_to([P, 4, P]),
                                    four(nmat[:, :])).then_inc(g_y, 1)
                merge_level(1)
                scores(2)
                scores(3)
                merge_level(2)
                y_add(0)
                scores(4)
                scores(5)
                lo(it + P_LOOP // RING, 2)
                merge_level(3)
                scores(6)
                scores(7)
                merge_level(4)
                lo(it + P_LOOP // RING, 3)
                y_add(1)
                merge_level(5)
                merge_level(6)
                dve.wait_ge(g_state, it + 1)
                dve.tensor_copy(o[:, 0, bass.ds(it * 256, 256)], ps[:, 4, 0:256]).then_inc(g_ocopy, 1)
                dve.wait_ge(g_ks, it + 1)
                for h in range(2):
                    ins = dve.scalar_tensor_tensor(resid[:, h, :], ps[:, 2, h * P:(h + 1) * P],
                                                   negc[:, bass.ds(it * 2 + h, 1)],
                                                   vtok[:, 1, bass.ds(it * 256 + h * P, P)], ALU.mult, ALU.add)
                ins.then_inc(g_r, 1)
                lo(it + (P_LOOP // RING + 1), 0)
                dve.wait_ge(g_o1, it + 1)
                dve.wait_ge(g_qs, it + 1)
                dve.tensor_tensor(o[:, 1, bass.ds(it * 256, 256)], ps[:, 4, 0:256], qs[:, :],
                                  ALU.add).then_inc(g_oadd, 1)
                lo(it + (P_LOOP // RING + 1), 1)

            dve.wait_ge(b_osq, 1)
            link(dve.tensor_reduce(stat[:, 0, 0:16], osq.rearrange("p (n d) -> p n d", d=P), AX_X, ALU.add))
            rsqrt(16, 1.0 / P, None)
            dve.wait_ge(g_oadd, GDN_HEADS // 2)
            o_heads = o.rearrange("p t c -> p (t c)").rearrange("p (n d) -> p n d", d=P)
            dve.tensor_tensor(o_heads, o_heads, stat[:, 1, 0:16].unsqueeze(2).broadcast_to([P, 16, P]),
                              ALU.mult).then_inc(b_red, 1)
            for i in range(N_ZGDN):
                lo(*divmod(P_ZGDN + i + 2, RING))
                if i % 2 == 1:
                    t = i // 2
                    dve.wait_ge(b_z, i + 1)
                    dve.tensor_tensor(xy[:, t, :], xy[:, t, :], z[:, t, :], ALU.mult).then_inc(b_yz, 1)
            dve.wait_ge(b_red, 1)
            dve.wait_ge(acc_free, 2 + N_ZG + N_ZGDN)
            for t in range(NT):
                dve.tensor_tensor(o[:, t, :], o[:, t, :], zg[:, t, :], ALU.mult).then_inc(b_o, 1)
            dve.wait_ge(b_gate, 4)
            dve.tensor_scalar(sq, sq, 0.5, 0.5, ALU.mult, ALU.add).then_inc(b_zg, 1)

            def back_lo(f):
                dve.wait_ge(bt_hi, f + 1)
                if f < 4:
                    dve.scalar_tensor_tensor(act_r[:, 1, 2 * f:2 * f + 2, :].rearrange("p a b -> p (a b)"),
                                             ps[:, 4 + f % 4, :], prm[:, Q_GDNN:Q_GDNN + 1],
                                             f32(act_r[:, 0, 2 * f:2 * f + 2, :].rearrange("p a b -> p (a b)")),
                                             ALU.mult, ALU.subtract).then_inc(bt_lo, 1)
                else:
                    for m in range(2):
                        a = 2 * (f - 4) + m
                        ins = dve.scalar_tensor_tensor(yt[:, 1, a, :], ps[:, 4 + f % 4, m * SEQ:(m + 1) * SEQ],
                                                       prm[:, Q_SSDN + a:Q_SSDN + a + 1], f32(yt[:, 0, a, :]),
                                                       ALU.mult, ALU.subtract)
                    ins.then_inc(bt_lo, 1)

            dve.wait_ge(b_yss, NT)
            rsqrt(NT, 1.0 / SSD_INNER, b_yr)
            for f in range(4):
                back_lo(f)

            def merge_gdn(i):
                p = P_WGDN + i
                dve.wait_ge(piece_mm, p + 1)
                dve.wait_ge(b_zg, 1)
                dve.tensor_tensor(merged[:, 2 * i:2 * i + 2, :], gates[:, 8 + 2 * i:10 + 2 * i, :],
                                  two(ps[:, p % 2, :]), ALU.mult).then_inc(b_m, 1)

            def merge_ssd(cb):
                dve.wait_ge(piece_mm, P_WSSD + 2 * cb + 2)
                if cb >= 1:
                    dve.wait_ge(b_m, 4 + cb)
                dve.tensor_tensor(mtmp[:, :, :], gates[:, 2 * cb:2 * cb + 2, :],
                                  ps[:, 2 * (cb % 2):2 * (cb % 2) + 2, 0:SEQ], ALU.mult).then_inc(b_mt, 1)
                dve.wait_ge(b_mt, cb + 1)
                dve.wait_ge(b_m, 4)
                dve.tensor_tensor(merged[:, 2 * cb:2 * cb + 2, :], merged[:, 2 * cb:2 * cb + 2, :],
                                  mtmp[:, :, :], ALU.add).then_inc(b_m, 1)

            merge_gdn(0)
            lo(*divmod(P_WGDN + 2, RING))
            for f in range(4, 8):
                back_lo(f)
            merge_gdn(1)
            lo(*divmod(P_WGDN + 3, RING))
            for f in range(8, 12):
                back_lo(f)
            for i in range(8):
                p = P_WSSD + i
                if i < 2:
                    merge_gdn(2 + i)
                lo(*divmod(p, RING))
                if i >= 2 and i % 2 == 1:
                    merge_ssd(i // 2 - 1)
            lo(*divmod(P_WOUT, RING))
            lo(*divmod(P_WOUT + 1, RING))
            merge_ssd(3)

            dve.wait_ge(b_mhi, 1)
            dve.wait_ge(b_m, 8)
            dve.tensor_tensor(act_r[:, 1, :, :], merged, f32(act_r[:, 0, :, :]), ALU.subtract).then_inc(b_mlo, 1)
            dve.wait_ge(s_xres, 16)
            for i in range(4):
                p = P_WOUT + i
                if i + 2 < 4:
                    lo(*divmod(p + 2, RING))
                dve.wait_ge(piece_mm, p + 1)
                dve.tensor_tensor(hres[:, :, i * COLS:(i + 1) * COLS], hres[:, :, i * COLS:(i + 1) * COLS],
                                  two(ps[:, p % 2, :]), ALU.add).then_inc(b_h, 1)

            dve.wait_ge(n_ss, NT)
            rsqrt(NT, 1.0 / D, None)
            dve.wait_ge(s_moep, 48)
            dve.wait_ge(b_h, 4)
            for t in range(NT):
                dve.scalar_tensor_tensor(u[:, t, :], hres[:, t, :], stat[:, 1, t:t + 1], ln2b[:, :],
                                         ALU.mult, ALU.mult).then_inc(n_u, 1)

            R = [rt[:, i, :, :] for i in range(24)]
            io4 = iota[:, 0:4].unsqueeze(1).broadcast_to([P, NT, 4])

            def col(i):
                return rt[:, i, :, 0:1]

            def wide(i):
                return rt[:, i, :, 0:1].broadcast_to([P, NT, 4])

            def first_max(src, best, onehot, scratch):
                link(dve.tensor_reduce(col(best), R[src], AX_X, ALU.max))
                link(dve.tensor_tensor(R[scratch], R[src], wide(best), ALU.is_equal))
                link(dve.scalar_tensor_tensor(R[scratch], R[scratch], -16.0, io4, ALU.mult, ALU.add))
                link(dve.tensor_reduce(col(onehot), R[scratch], AX_X, ALU.min))
                link(dve.tensor_copy(col(scratch + 1), col(onehot)))
                link(dve.tensor_tensor(R[onehot], R[scratch], wide(scratch + 1), ALU.is_equal))

            dve.wait_ge(b_mlo, 1)
            dve.wait_ge(n_utc, 4)
            dve.memset(ps[:, 4, :], 0.0).then_inc(e_zero, 1)
            dve.memset(ps[:, 5, :], 0.0).then_inc(e_zero, 1)
            dve.memset(f32(selt[:, :, :]), 0.0).then_inc(e_back, 1)
            dve.wait_ge(n_log, 1)
            link(dve.tensor_tensor(rl[:, :, :], ps[:, 0, 0:40].rearrange("p (t c) -> p t c", t=NT),
                                   row[:, R_BG:R_END].unsqueeze(1).broadcast_to([P, NT, 20]), ALU.add))
            link(dve.tensor_copy(R[0], rl[:, :, 0:4]))
            first_max(0, 1, 2, 20)
            dve.tensor_tensor(R[3], R[0], wide(1), ALU.subtract).then_inc(n_lg, 1)
            grp = rl[:, :, 4:20].rearrange("p t (g e) -> p t g e", g=GROUPS)
            re4 = re[:, :, :].rearrange("p t (g e) -> p t g e", g=GROUPS)
            link(dve.tensor_tensor(re4, grp, R[2].unsqueeze(3).broadcast_to([P, NT, GROUPS, EXPERTS]), ALU.mult))
            link(dve.tensor_reduce(R[6], re[:, :, :].rearrange("p t (g e) -> p t e g", g=GROUPS), AX_X, ALU.add))
            first_max(6, 7, 8, 20)
            link(dve.scalar_tensor_tensor(R[9], R[8], -1e30, R[6], ALU.mult, ALU.add))
            first_max(9, 10, 11, 20)
            dve.tensor_tensor(col(15), col(10), col(7), ALU.subtract).then_inc(n_lg, 1)
            link(dve.tensor_tensor(R[12], rt[:, 2, 0, :].unsqueeze(1).broadcast_to([P, NT, 4]),
                                   rt[:, 2, 1, :].unsqueeze(1).broadcast_to([P, NT, 4]), ALU.add))
            dve.memset(rinfo[:, :], 0.0).then_inc(n_oh, 1)
            dve.wait_ge(n_exp, 2)
            link(dve.tensor_reduce(col(5), R[4], AX_X, ALU.add))
            link(dve.tensor_scalar(col(13), col(16), 1.0, None, ALU.add))
            link(dve.tensor_tensor(col(14), col(5), col(13), ALU.mult))
            link(dve.reciprocal(col(17), col(14)))
            link(dve.tensor_tensor(col(18), col(17), col(16), ALU.mult))
            link(dve.tensor_tensor(R[19], R[8], wide(17), ALU.mult))
            link(dve.tensor_tensor(R[20], R[11], wide(18), ALU.mult))
            link(dve.tensor_tensor(cw[:, :, :], R[19], R[20], ALU.add))
            link(dve.memset(qsl[:, :, :], -1.0))
            dve.wait_ge(n_cnt, 1)
            link(dve.tensor_tensor(R[21], ps[:, 1, 0:8].rearrange("p (t g) -> p t g", t=NT), R[2], ALU.mult))
            link(dve.tensor_scalar(qsl[:, :, 0:4], R[21], -1.0, None, ALU.add))
            link(dve.tensor_reduce(col(22), R[21], AX_X, ALU.add))
            link(dve.tensor_scalar(qsl[:, :, 4:5], col(22), -1.0 - P, None, ALU.add))
            link(dve.tensor_scalar(rinfo[:, 0:4], ps[:, 1, 8:12], float(P), None, ALU.is_gt))
            link(dve.tensor_reduce(rinfo[:, 4:5], rinfo[:, 0:4], AX_X, ALU.add))
            link(dve.tensor_scalar(rinfo[:, 6:7], rinfo[:, 4:5], float(GROUPS), None, ALU.add))
            link(dve.tensor_tensor(rinfo[:, 0:4], rinfo[:, 0:4], iota[:, 0:4], ALU.mult))
            link(dve.tensor_reduce(rinfo[:, 7:8], rinfo[:, 0:4], AX_X, ALU.add))
            dve.tensor_copy(rint[:, :], rinfo[:, 6:8]).then_inc(n_route, 1)
            dve.wait_ge(n_route, 1)
            runs = dve.value_load(rint[0:1, 0:1], min_val=GROUPS, max_val=GROUPS + 1)

            def select(it):
                for t in range(NT):
                    ins = dve.tensor_scalar(sel[:, t, :], iota, qsl[:, t, bass.ds(it, 1)], None, ALU.is_equal)
                ins.then_inc(e_sel, 1)

            def x_low(it):
                dve.wait_ge(e_gath, it + 1)
                dve.tensor_copy(cslot[:, :], ps[:, 7, 0:EXPERTS])
                dve.wait_ge(e_xhi, it + 1)
                dve.tensor_tensor(xg[:, 1, :, :].rearrange("p k s -> p (k s)"),
                                  ps[:, 0:2, :].rearrange("p a b -> p (a b)"),
                                  f32(xg[:, 0, :, :].rearrange("p k s -> p (k s)")), ALU.subtract).then_inc(e_xlo, 1)

            def y_low(it):
                dve.wait_ge(e_yhi, it + 1)
                dve.tensor_tensor(ysp[:, 1, :], ps[:, 4:6, :].rearrange("p a b -> p (a b)"), f32(ysp[:, 0, :]),
                                  ALU.subtract).then_inc(e_ylo, 1)

            def y_add_back(it, t):
                dve.wait_ge(e_scat, it * NT + (t + 1))
                dve.tensor_tensor(hres[:, t, :], hres[:, t, :],
                                  ps[:, 4:6, :].rearrange("p a b -> p (a b)"), ALU.add).then_inc(e_add, 1)

            select(0)
            x_low(0)
            with dve.Fori(0, runs) as it:
                def mlo(n):
                    dve.wait_ge(hi_done, it * MOE_PIECES + (N_MIX + n + 1))
                    dve.tensor_tensor(los[n % MOE_RING], mring[n % MOE_RING], f32(his[n % MOE_HI]),
                                      ALU.subtract).then_inc(lo_done, 1)

                mlo(0)
                mlo(1)
                y_low(it)
                mlo(2)
                dve.wait_ge(e_xlo, it + 1)
                for n, (kind, e, half) in enumerate(ORDER):
                    if n == SCATTER_0:
                        y_add_back(it, 0)
                        dve.wait_ge(e_add, it * 2 + 1)
                    if n == SCATTER_1:
                        y_add_back(it, 1)
                        dve.wait_ge(e_add, it * 2 + 2)
                    if n + 3 < MOE_PIECES:
                        mlo(n + 3)
                    if (kind, half) == ("up", 1):
                        dve.wait_ge(e_silu, it * EXPERTS + (e + 1))
                        dve.wait_ge(piece_mm, it * MOE_PIECES + (N_MIX + n + 1))
                        dve.scalar_tensor_tensor(hbuf[:, e % 2, :], sgate, cslot[:, e:e + 1],
                                                 ps[:, 2 * (e % 2) + 1, :], ALU.mult, ALU.mult).then_inc(e_h, 1)
                    if n + 1 in TURN_H:
                        d = TURN_H[n + 1]
                        dve.wait_ge(e_hthi, it * EXPERTS + (d + 1))
                        dve.tensor_tensor(ht[:, d % 2, 1, :, :].rearrange("p a b -> p (a b)"), ps[:, 6, :],
                                          f32(ht[:, d % 2, 0, :, :].rearrange("p a b -> p (a b)")),
                                          ALU.subtract).then_inc(e_htlo, 1)
                    if n == TURN_SEL:
                        dve.wait_ge(e_turn, it + 1)
                        dve.wait_ge(e_gath, it + 1)
                        select(it + 1)
                    if n + 1 == NEXT_GROUP:
                        dve.wait_ge(e_h, it * EXPERTS + EXPERTS)
                        x_low(it + 1)
            y_low(runs)
            for t in range(NT):
                y_add_back(runs, t)

            dve.wait_ge(f_ss, NT)
            rsqrt(NT, 1.0 / D, None)
            for t in range(NT):
                dve.scalar_tensor_tensor(u[:, t, :], hres[:, t, :], stat[:, 1, t:t + 1], finb[:, :],
                                         ALU.mult, ALU.mult).then_inc(f_out, 1)

        @block.gpsimd
        def _(pool):
            pool.wait_ge(evac_a, 12 + GDN_HEADS)
            pool.wait_ge(s_cst, 64)
            pool.wait_ge(dec_v, 1)
            with pool.Fori(0, GDN_HEADS // 2) as it:
                def ssd_rhs(k):
                    if k >= 2:
                        pool.wait_ge(m_seg, it * 8 + (k - 1))
                    for part, v in enumerate((f32(vdec_h[:, :, :]), vdec_l[:, :, :])):
                        pool.tensor_tensor(ssdrhs[:, k % 2, part, 0:256], causal2,
                                           v[:, 0, bass.ds(it * 8 + k, 1)].broadcast_to([P, 256]), ALU.mult)
                        ins = pool.tensor_tensor(ssdrhs[:, k % 2, part, 256:384], causal,
                                                 v[:, 1, bass.ds(it * 8 + k, 1)].broadcast_to([P, P]), ALU.mult)
                    ins.then_inc(m_rhs, 1)

                def xd_in(k):
                    return xy[:, :, bass.ds(it * 512 + k * 256, 256)].rearrange("p t (h d) -> p t h d", h=4)

                def xd_d(k):
                    return row[:, bass.ds(it * 8 + (R_D + 4 * k), 4)].unsqueeze(1).unsqueeze(3)\
                        .broadcast_to([P, NT, 4, SSD_HD])

                pool.tensor_copy(kq_h, kqt[:, bass.ds(it * 2, 2), :].rearrange("p a b -> p (a b)"))\
                    .then_inc(g_staged, 1)
                for part, v in enumerate((f32(vdec_h[:, :, :]), vdec_l[:, :, :])):
                    for h in range(2):
                        for c in range(NT):
                            n = 2 * h + c
                            ins = pool.tensor_tensor(
                                gdnrhs[:, part, n * P:(n + 1) * P], causal,
                                v[:, c, bass.ds(it * 2 + (SSD_HEADS + h), 1)].broadcast_to([P, P]), ALU.mult)
                ins.then_inc(g_rhs, 1)
                ssd_rhs(0)
                ssd_rhs(1)
                for dst in (inv, invt):
                    pool.tensor_copy(four(dst), ident.unsqueeze(1).broadcast_to([P, 4, P])).then_inc(g_eye, 1)
                pool.wait_ge(g_exp, it + 1)
                pool.tensor_tensor(four(gdecm[:, :]), four(gdec[:, :]), causal.unsqueeze(1).broadcast_to([P, 4, P]),
                                   ALU.mult).then_inc(g_mask, 1)
                for t in range(NT):
                    ins = pool.tensor_tensor(xd[:, t, :, :], xd_in(0)[:, t], xd_d(0)[:, t], ALU.mult)
                ins.then_inc(m_xd, 1)
                ssd_rhs(2)
                ssd_rhs(3)
                ssd_rhs(4)
                ssd_rhs(5)
                pool.wait_ge(m_ydone, it * 2 + 1)
                for t in range(NT):
                    ins = pool.tensor_tensor(xd[:, t, :, :], xd_in(1)[:, t], xd_d(1)[:, t], ALU.mult)
                ins.then_inc(m_xd, 1)
                ssd_rhs(6)
                ssd_rhs(7)
                pool.wait_ge(m_seg, it * 8 + 8)
                pool.wait_ge(m_ydone, it * 2 + 2)
                pool.wait_ge(g_oadd, it + 1)

        @block.tensor
        def _(pe):
            def triple(dst, w_hi, w_lo, a_hi, a_lo, start, stop, stationary):
                if stationary == "w":
                    pe.matmul(dst, w_hi, a_hi, start=start, stop=False)
                    pe.matmul(dst, w_hi, a_lo, start=False, stop=False)
                    return pe.matmul(dst, w_lo, a_hi, start=False, stop=stop)
                pe.matmul(dst, a_hi, w_hi, start=start, stop=False)
                pe.matmul(dst, a_hi, w_lo, start=False, stop=False)
                return pe.matmul(dst, a_lo, w_hi, start=False, stop=stop)

            def cm_step(p, m, k, dst, a, start, stop, slots=2):
                h, l = parts(p, slots)
                cols = slice(m * P, (m + 1) * P)
                return triple(dst, h[:, k, cols], l[:, k, cols], a[0], a[1], start, stop, "w")

            def tm_step(p, t, k, dst, start, stop):
                h, l = parts(p, 2)
                toks = slice(t * P, (t + 1) * P)
                return triple(dst, h[:, k, :], l[:, k, :], act_r[:, 0, k, toks], act_r[:, 1, k, toks], start, stop,
                              "a")

            def parts(p, slots):
                views = (his[p % slots], los[p % RING])
                return [v.rearrange("p (k c) -> p k c", k=KC) for v in views]

            pe.wait_ge(s_cst, 64)
            for t in range(NT):
                pe.wait_ge(xn_done, t + 1)
            for b in range(4):
                for k in (2 * b, 2 * b + 1):
                    for t in range(NT):
                        ins = pe.transpose(ps[:, 2 + b, (k % 2) * SEQ + t * P:(k % 2) * SEQ + (t + 1) * P],
                                           xn[:, t, k * P:(k + 1) * P], ident)
                ins.then_inc(xt_mm, 1)
            pe.wait_ge(sml_lo, 1)
            pe.wait_ge(xt_lo, KC)
            for t in range(NT):
                for k in range(KC):
                    w = slice(k * SMALL, (k + 1) * SMALL)
                    ins = triple(ps[:, 6, t * SMALL:(t + 1) * SMALL], sml_h[:, w], sml_l[:, w],
                                 act_r[:, 0, k, t * P:(t + 1) * P], act_r[:, 1, k, t * P:(t + 1) * P],
                                 k == 0, k == KC - 1, "a")
            ins.then_inc(sml_mm, 1)

            def conv_piece(p, j):
                pe.wait_ge(lo_done, p + 1)
                if not (isinstance(p, int) and p < RING):
                    pe.wait_ge(tap_step, p * 6 - 18)
                for m in range(2):
                    for k in range(KC):
                        ins = cm_step(j, m, k, ps[:, j, m * SEQ:(m + 1) * SEQ], (act_r[:, 0, k, :], act_r[:, 1, k, :]),
                                      k == 0, k == KC - 1, RING)
                ins.then_inc(piece_mm, 1)

            for j in range(RING):
                conv_piece(j, j)
            with pe.Fori(1, N_CONV // RING) as q:
                for j in range(RING):
                    conv_piece(q * RING + j, j)

            def turn_fill(what, i, first_tile):
                f = fill_no[what, i]
                if f >= 6:
                    wait_evac(pe, f - 6)
                t, b = i % NT, i // NT
                for m in range(4):
                    ins = pe.transpose(bank(f)[:, m * P:(m + 1) * P],
                                       cv[:, first_tile + 4 * b + m, t * P:(t + 1) * P], ident)
                ins.then_inc(fill_mm, 1)

            pe.wait_ge(silu_done, N_CONV)
            for i in range(4):
                turn_fill("v", i, 16)
            pe.wait_ge(sq_done, 4)
            pe.wait_ge(tap_step, 6 * N_CONV)
            for t in range(NT):
                for c in range(16):
                    ins = pe.matmul(ps[:, 1, t * 16 + c:t * 16 + c + 1], sq[:, c * SEQ + t * P:c * SEQ + (t + 1) * P],
                                    ones[:, 0:1], start=True, stop=True)
            ins.then_inc(ss_mm, 1)
            for i in range(8):
                turn_fill("x", i, 24)
            pe.wait_ge(dec_v, 1)
            for t in range(NT):
                pe.matmul(ps[:, 0, t * 8:(t + 1) * 8], causal, vdec[:, t, SSD_HEADS:], start=True, stop=True)
            pe.matmul(ps[:, 0, 16:24], strict, vdec[:, 0, SSD_HEADS:], start=True, stop=True).then_inc(dec_mm, 1)
            for i in range(SSD_GROUPS):
                f = fill_no["cb", i]
                wait_evac(pe, f - 6)
                pe.matmul(bank(f)[:, 0:SEQ], cv[:, 40 + i, 0:P], cv[:, 44 + i, :], start=True, stop=True)
                pe.matmul(bank(f)[:, SEQ:SEQ + P], cv[:, 40 + i, P:SEQ], cv[:, 44 + i, P:SEQ],
                          start=True, stop=True).then_inc(fill_mm, 1)
            for what, first_tile in (("k", 8), ("q", 0)):
                for i in range(4):
                    turn_fill(what, i, first_tile)
            pe.wait_ge(evac_d, 12)
            for i in range(GDN_HEADS):
                f = fill_no["kqt", i]
                wait_evac(pe, f - 6)
                for c in range(NT):
                    kk = ktok[:, i * P:(i + 1) * P] if c == 0 else knorm1[:, i * P:(i + 1) * P]
                    pe.transpose(bank(f)[:, c * 256:c * 256 + P], kk, ident)
                    ins = pe.transpose(bank(f)[:, c * 256 + P:(c + 1) * 256], qn[:, c, i * P:(i + 1) * P], ident)
                ins.then_inc(fill_mm, 1)
            pe.wait_ge(evac_a, 12 + GDN_HEADS)
            pe.wait_ge(tab_done, 2)
            pe.wait_ge(cst_r, 3)

            with pe.Fori(0, GDN_HEADS // 2) as it:
                done = [0]

                def stream(steps):
                    for _ in range(steps):
                        j, s = divmod(done[0], 16)
                        m, k = divmod(s, KC)
                        if s == 0:
                            pe.wait_ge(lo_done, it * 4 + (P_LOOP + j + 1))
                            pe.wait_ge(acc_free, it * 4 + (j + 1))
                        dst = ps[:, j % 2, m * SEQ:(m + 1) * SEQ]
                        if j % 2 == 0:
                            ins = tm_step(j, m, k, dst, k == 0, k == KC - 1)
                        else:
                            ins = cm_step(j, m, k, dst, (act_r[:, 0, k, :], act_r[:, 1, k, :]), k == 0, k == KC - 1)
                        if s == 15:
                            ins.then_inc(piece_mm, 1)
                        done[0] += 1

                def segments(k):
                    pe.wait_ge(m_rhs, it * 8 + (k + 1))
                    if k >= 2:
                        pe.wait_ge(m_exp, it * 8 + (k - 1))
                    dst = ps[:, 5 + k % 2, :]
                    for part in range(2):
                        pe.matmul(dst[:, 0:384], strict_r[:, :], ssdrhs[:, k % 2, part, :], start=(part == 0),
                                  stop=False)
                    for part in range(2):
                        ins = pe.matmul(dst[:, P:2 * P], ones_r[:, :], ssdrhs[:, k % 2, part, 256:384], start=False,
                                        stop=(part == 1))
                    ins.then_inc(m_seg, 1)

                def ssd_out(k):
                    pe.wait_ge(m_gl, it * 8 + (k + 1))
                    if k == 4:
                        pe.wait_ge(m_ydone, it * 2 + 1)
                    c = (k % 4) * SSD_HD
                    xs = [xy[:, t, bass.ds(it * 512 + k * SSD_HD, SSD_HD)] for t in range(NT)]
                    pe.matmul(ps[:, 7, c:c + SSD_HD], ldec[:, k % 2, 0:P], xs[0], start=True, stop=True)
                    pe.matmul(ps[:, 7, 256 + c:256 + c + SSD_HD], ldec[:, k % 2, P:2 * P], xs[0], start=True,
                              stop=False)
                    pe.matmul(ps[:, 7, 256 + c:256 + c + SSD_HD], ldec[:, k % 2, 2 * P:3 * P], xs[1], start=False,
                              stop=True).then_inc(m_y, 1)

                def four_mm(b, lhs, rhs, done_sem):
                    for n in range(4):
                        c = slice(n * P, (n + 1) * P)
                        ins = pe.matmul(ps[:, b, c], lhs[:, c], rhs[:, c], start=True, stop=True)
                    ins.then_inc(done_sem, 1)

                pe.wait_ge(g_staged, it + 1)
                for h in range(2):
                    for c in range(NT):
                        a = (2 * h + c) * 256
                        ins = pe.matmul(ps[:, 2 + h, c * 256:(c + 1) * 256], kq_h[:, a:a + P], kq_h[:, a:a + 256],
                                        start=True, stop=True)
                ins.then_inc(g_kq, 1)
                pe.wait_ge(g_rhs, it + 1)
                for part in range(2):
                    ins = pe.matmul(ps[:, 4, :], strict_r[:, :], gdnrhs[:, part, :], start=(part == 0),
                                    stop=(part == 1))
                ins.then_inc(g_seg, 1)
                stream(3)
                segments(0)
                segments(1)
                stream(3)
                pe.wait_ge(g_nt, it + 1)
                for n in range(4):
                    ins = pe.transpose(ps[:, 4, n * P:(n + 1) * P], nmat[:, n * P:(n + 1) * P], ident)
                ins.then_inc(g_ntt, 1)
                stream(3)
                pe.wait_ge(g_aqk, it + 1)
                for l in range(1, 7):
                    pe.wait_ge(g_x, it * 6 + l)
                    four_mm(2, nmat, inv, g_p)
                    if l <= 4:
                        ssd_out(2 * l - 2)
                        if l <= 3:
                            segments(2 * l)
                    stream(3)
                    pe.wait_ge(g_ps, it * 6 + l)
                    pe.wait_ge(g_y, it * 7 + l)
                    if l < 6:
                        four_mm(3, invt, pmat, g_xp)
                    four_mm(4, pmat, invt, g_yp)
                    if l <= 4:
                        ssd_out(2 * l - 1)
                        if l <= 3:
                            segments(2 * l + 1)
                    stream(3)
                vt = [[vtok[:, c, bass.ds(it * 256 + h * P, P)] for h in range(2)] for c in range(NT)]
                pe.wait_ge(g_y, it * 7 + 7)
                for h in range(2):
                    ins = pe.matmul(ps[:, 2, h * P:(h + 1) * P], invt[:, 2 * h * P:(2 * h + 1) * P], vt[0][h],
                                    start=True, stop=True)
                ins.then_inc(g_solve, 1)
                stream(4)
                pe.wait_ge(g_vn, it * 2 + 1)
                pe.wait_ge(g_kd, it + 1)
                for h in range(2):
                    pe.matmul(ps[:, 3, h * P:(h + 1) * P], kd[:, h, :], vnew[:, 0, h, :], start=True, stop=True)
                    ins = pe.matmul(ps[:, 4, h * P:(h + 1) * P], aqk[:, 2 * h * P:(2 * h + 1) * P], vnew[:, 0, h, :],
                                    start=True, stop=True)
                ins.then_inc(g_state, 1)
                stream(4)
                pe.wait_ge(g_scopy, it + 1)
                for h in range(2):
                    a = (2 * h + 1) * 256
                    pe.matmul(ps[:, 2, h * P:(h + 1) * P], kq_h[:, a:a + P], s1[:, h * P:(h + 1) * P],
                              start=True, stop=True)
                    ins = pe.matmul(ps[:, 3, h * P:(h + 1) * P], kq_h[:, a + P:a + 256], s1[:, h * P:(h + 1) * P],
                                    start=True, stop=True)
                ins.then_inc(g_ks, 1)
                stream(4)
                pe.wait_ge(g_r, it + 1)
                for h in range(2):
                    ins = pe.matmul(ps[:, 2, h * P:(h + 1) * P], invt[:, (2 * h + 1) * P:(2 * h + 2) * P],
                                    resid[:, h, :], start=True, stop=True)
                ins.then_inc(g_solve, 1)
                stream(4)
                pe.wait_ge(g_vn, it * 2 + 2)
                pe.wait_ge(g_ocopy, it + 1)
                for h in range(2):
                    ins = pe.matmul(ps[:, 4, h * P:(h + 1) * P], aqk[:, (2 * h + 1) * P:(2 * h + 2) * P],
                                    vnew[:, 1, h, :], start=True, stop=True)
                ins.then_inc(g_o1, 1)
                stream(3)
                pe.wait_ge(g_oadd, it + 1)
                assert done[0] == 64

            for i in range(N_ZGDN):
                p = P_ZGDN + i
                pe.wait_ge(lo_done, p + 1)
                pe.wait_ge(acc_free, p - P_LOOP + 1)
                for t in range(NT):
                    for k in range(KC):
                        ins = tm_step(p, t, k, ps[:, p % 2, t * SEQ:(t + 1) * SEQ], k == 0, k == KC - 1)
                ins.then_inc(piece_mm, 1)

            def back_fill(f):
                if f >= 4:
                    pe.wait_ge(bt_lo, f - 3)
                for m in range(2):
                    for t in range(NT):
                        a = 2 * f + m if f < 4 else 2 * (f - 4) + m
                        src = o if f < 4 else xy
                        ins = pe.transpose(ps[:, 4 + f % 4, m * SEQ + t * P:m * SEQ + (t + 1) * P],
                                           src[:, t, a * P:(a + 1) * P], ident)
                ins.then_inc(bt_mm, 1)

            def gdn_piece(i):
                p = P_WGDN + i
                pe.wait_ge(lo_done, p + 1)
                if i < 2:
                    pe.wait_ge(acc_free, 2 + N_ZG + N_ZGDN)
                else:
                    pe.wait_ge(b_m, i - 1)
                for m in range(2):
                    for k in range(KC):
                        ins = cm_step(p, m, k, ps[:, p % 2, m * SEQ:(m + 1) * SEQ],
                                      (act_r[:, 0, k, :], act_r[:, 1, k, :]), k == 0, k == KC - 1)
                ins.then_inc(piece_mm, 1)

            pe.wait_ge(b_o, NT)
            for f in range(4):
                back_fill(f)
            pe.wait_ge(bt_lo, 4)
            gdn_piece(0)
            pe.wait_ge(b_ys, NT)
            for f in range(4, 8):
                back_fill(f)
            gdn_piece(1)
            for f in range(8, 12):
                back_fill(f)
            gdn_piece(2)
            gdn_piece(3)
            pe.wait_ge(bt_lo, 12)
            for cb in range(4):
                for half in range(2):
                    p = P_WSSD + 2 * cb + half
                    pe.wait_ge(lo_done, p + 1)
                    if half == 0:
                        pe.wait_ge(b_m, 4 if cb < 2 else 3 + cb)
                    for m in range(2):
                        for k in range(KC):
                            a = half * KC + k
                            ins = cm_step(p, m, k, ps[:, 2 * (cb % 2) + m, 0:SEQ],
                                          (yt[:, 0, a, :], yt[:, 1, a, :]), a == 0, a == 2 * KC - 1)
                    ins.then_inc(piece_mm, 1)
            pe.wait_ge(b_mlo, 1)
            for i in range(4):
                p = P_WOUT + i
                pe.wait_ge(lo_done, p + 1)
                if i >= 2:
                    pe.wait_ge(b_h, i - 1)
                for t in range(NT):
                    for k in range(KC):
                        ins = tm_step(p, t, k, ps[:, p % 2, t * SEQ:(t + 1) * SEQ], k == 0, k == KC - 1)
                ins.then_inc(piece_mm, 1)

            pe.wait_ge(n_u, NT)
            for f in range(4):
                for k in (2 * f, 2 * f + 1):
                    for t in range(NT):
                        ins = pe.transpose(ps[:, 4 + f, (k % 2) * SEQ + t * P:(k % 2) * SEQ + (t + 1) * P],
                                           u[:, t, k:D:KC], ident)
                ins.then_inc(n_ut, 1)
            pe.wait_ge(n_utc, 4)
            pe.wait_ge(s_moep, 48)
            for t in range(NT):
                for k in range(KC):
                    ins = pe.matmul(ps[:, 0, t * 20:(t + 1) * 20], ut[:, k, t * P:(t + 1) * P],
                                    wr[:, k * 20:(k + 1) * 20], start=(k == 0), stop=(k == KC - 1))
            ins.then_inc(n_log, 1)
            pe.wait_ge(n_oh, 1)
            pe.matmul(ps[:, 1, 0:4], causal, rt[:, 2, 0, :], start=True, stop=True)
            pe.matmul(ps[:, 1, 4:8], ones, rt[:, 2, 0, :], start=True, stop=False)
            pe.matmul(ps[:, 1, 4:8], causal, rt[:, 2, 1, :], start=False, stop=True)
            pe.matmul(ps[:, 1, 8:12], ones, rt[:, 12, 0, :], start=True, stop=True).then_inc(n_cnt, 1)
            pe.wait_ge(n_route, 1)
            runs = pe.value_load(rint[0:1, 0:1], min_val=GROUPS, max_val=GROUPS + 1)

            def gather(it):
                pe.wait_ge(e_sel, it + 1)
                for k in range(KC):
                    for t in range(NT):
                        pe.matmul(ps[:, k // 4, (k % 4) * P:(k % 4 + 1) * P], u[:, t, k:D:KC], sel[:, t, :],
                                  start=(t == 0), stop=(t == 1))
                for t in range(NT):
                    ins = pe.matmul(ps[:, 7, 0:EXPERTS], sel[:, t, :], cw[:, t, :], start=(t == 0), stop=(t == 1))
                ins.then_inc(e_gath, 1)

            def scatter(it, t):
                pe.wait_ge(e_yhi, it + 1)
                pe.wait_ge(e_ylo, it + 1)
                pe.wait_ge(e_back, it + 1)
                if t > 0:
                    pe.wait_ge(e_add, it * NT + t)
                for c in range(2):
                    for part in range(2):
                        ins = pe.matmul(ps[:, 4 + c, :], selt[:, t, :], ysp[:, part, c * 512:(c + 1) * 512],
                                        start=(part == 0), stop=(part == 1))
                ins.then_inc(e_scat, 1)

            gather(0)
            with pe.Fori(0, runs) as it:
                pe.wait_ge(e_xhi, it + 1)
                pe.wait_ge(e_xlo, it + 1)
                for n, (kind, e, half) in enumerate(ORDER):
                    if n == SCATTER_0:
                        scatter(it, 0)
                    if n == SCATTER_1:
                        scatter(it, 1)
                    if n in TURN_H:
                        d = TURN_H[n]
                        pe.wait_ge(e_h, it * EXPERTS + (d + 1))
                        for f in range(4):
                            ins = pe.transpose(ps[:, 6, f * P:(f + 1) * P], hbuf[:, d % 2, f:FF:4], ident)
                        ins.then_inc(e_ht, 1)
                    if n == TURN_SEL:
                        for t in range(NT):
                            ins = pe.transpose(ps[:, 7, (t + 1) * P:(t + 2) * P], sel[:, t, :], ident)
                        ins.then_inc(e_turn, 1)
                    if n == NEXT_GROUP:
                        pe.wait_ge(e_back, it + 2)
                        gather(it + 1)
                    if (kind, half) == ("down", 0):
                        pe.wait_ge(e_hthi, it * EXPERTS + (e + 1))
                        pe.wait_ge(e_htlo, it * EXPERTS + (e + 1))
                        if e == 0:
                            pe.wait_ge(e_add, it * NT + NT)
                    pe.wait_ge(lo_done, it * MOE_PIECES + (N_MIX + n + 1))
                    h, l = his[n % MOE_HI], los[n % MOE_RING]
                    if kind == "down":
                        for f in range(2):
                            for c in range(2):
                                w = slice(f * D + c * 512, f * D + (c + 1) * 512)
                                a = 2 * half + f
                                ins = triple(ps[:, 4 + c, :], h[:, w], l[:, w], ht[:, e % 2, 0, a, :],
                                             ht[:, e % 2, 1, a, :], e == 0 and a == 0, e == EXPERTS - 1 and a == 3,
                                             "a")
                    else:
                        for k in range(4):
                            w = slice(k * FF, (k + 1) * FF)
                            a = 4 * half + k
                            ins = triple(ps[:, 2 * (e % 2) + (kind == "up"), :], h[:, w], l[:, w], xg[:, 0, a, :],
                                         xg[:, 1, a, :], a == 0, a == KC - 1, "a")
                    ins.then_inc(piece_mm, 1)
            for t in range(NT):
                scatter(runs, t)


def constants():
    i = np.arange(P)
    causal = (i[:, None] <= i[None, :]).astype(np.float32)
    cst = np.concatenate([
        np.eye(P, dtype=np.float32), (i[:, None] > i[None, :]).astype(np.float32), causal,
        np.ones((P, P), np.float32), causal, np.tile(i.astype(np.float32), (P, 1))], axis=1)
    masks = np.zeros((P, 2, LEVELS, P), np.float32)
    for l in range(LEVELS):
        b = i >> l
        pair = (b[:, None] % 2 == 1) & (b[None, :] == b[:, None] - 1)
        masks[:, 0, l, :] = pair
        masks[:, 1, l, :] = pair.T
    return cst, masks.reshape(P, -1)


def cut_columns(w, halves=1):
    rows, cols = w.shape
    w = w.reshape(halves, KC, P, cols // COLS, COLS).transpose(3, 0, 2, 1, 4)
    return w.reshape(-1, P, PIECE)


def kernel(x, ln1_w, w_in, ssd_conv_w, ssd_conv_b, ssd_dt_bias, ssd_a_log, ssd_d, ssd_norm_w, w_ssd_proj,
           gdn_conv_w, gdn_dt_bias, gdn_a_log, gdn_norm_w, w_gdn_proj, b_merge, w_out, ln2_w,
           moe_w_group, moe_b_group, moe_w_expert, moe_b_expert, moe_w_gate, moe_w_up, moe_w_down,
           final_norm_w):
    import concourse.bacc as bacc
    from concourse.bass_utils import run_bass_kernel_spmd

    a = np.asarray
    w = a(w_in)[0]
    z_w, xbc_w, dt_w, qkv_w, ab_w, zg_w, gate_w = np.split(w, [2048, 5120, 5152, 8224, 8240, 9264], axis=1)
    zc, gc = cut_columns(z_w), cut_columns(gate_w)
    loop = np.stack([zc, gc], axis=1).reshape(-1, P, PIECE)
    mix = np.concatenate([cut_columns(qkv_w), cut_columns(xbc_w), loop, cut_columns(zg_w),
                          cut_columns(a(w_gdn_proj)[0]), cut_columns(a(w_ssd_proj)[0], 2),
                          cut_columns(a(w_out)[0])])
    small = np.concatenate([dt_w, ab_w], axis=1).reshape(KC, P, SMALL).transpose(1, 0, 2).reshape(P, KC * SMALL)
    conv = np.concatenate([a(gdn_conv_w)[0], a(ssd_conv_w)[0]], axis=1)
    bias = np.concatenate([np.zeros(3072, np.float32), a(ssd_conv_b)[0]])[None]
    conv = np.concatenate([conv, bias]).reshape(5, 48, P).transpose(2, 1, 0).reshape(P, 240)
    params = np.concatenate([conv, a(b_merge)[0].reshape(16, P).T, a(ln1_w)[0].reshape(KC, P).T,
                             a(ssd_norm_w)[0].reshape(16, P).T, a(gdn_norm_w)[0].reshape(1, P).T], axis=1)
    rows = np.concatenate([a(ssd_dt_bias)[0], a(gdn_dt_bias)[0], a(ssd_a_log)[0], a(gdn_a_log)[0], a(ssd_d)[0],
                           a(moe_b_group)[0], a(moe_b_expert)[0]])
    router = np.concatenate([a(moe_w_group)[0], a(moe_w_expert)[0]], axis=1).reshape(P, KC * 20)
    cst, masks = constants()
    arrays = {
        "w_mix": mix, "w_small": small, "w_router": router,
        "w_gate": a(moe_w_gate)[0].reshape(16, P, 2 * PIECE), "w_up": a(moe_w_up)[0].reshape(16, P, 2 * PIECE),
        "w_down": a(moe_w_down)[0].reshape(16, P, 2 * PIECE), "x": a(x), "consts": cst, "masks": masks,
        "params": params, "rows": rows, "ln2": a(ln2_w)[0], "final_w": a(final_norm_w),
    }
    arrays = {k: np.ascontiguousarray(v) for k, v in arrays.items()}
    nc = bacc.Bacc("TRN2", target_bir_lowering=False, num_devices=1)
    args = {k: nc.dram_tensor(k, v.shape, mybir.dt.from_np(v.dtype), kind="ExternalInput").ap()
            for k, v in arrays.items()}
    out = nc.dram_tensor("out", (1, SEQ, D), F32, kind="ExternalOutput").ap()
    hybrid_layer(nc, out=out, **args)
    r = run_bass_kernel_spmd(nc, [arrays], core_ids=[0])
    return r.results[0]["out"]
```

```python
from contextlib import ExitStack

import numpy as np

import concourse.bass as bass
from concourse import mybir

F32 = mybir.dt.float32
F32R = mybir.dt.float32r
I32 = mybir.dt.int32
U8 = mybir.dt.uint8
ALU = mybir.AluOpType
ACT = mybir.ActivationFunctionType
AX_X = mybir.AxisListType.X

P = 128
D = 1024
SEQ = 256
NT = SEQ // P
KC = D // P
EPS = 1e-6

SSD_INNER = 2048
SSD_HEADS = 32
SSD_HD = 64
SSD_GROUPS = 4
SSD_XBC = 3072
GDN_HEADS = 8
GDN_DIM = 1024
SMALL = SSD_HEADS + 2 * GDN_HEADS
DECAYS = SSD_HEADS + GDN_HEADS
LEVELS = 7

GROUPS = 4
EXPERTS = 4
FF = 512

PIECE = 2048
COLS = PIECE // KC

N_QKV, N_XBC, N_TURN, N_LOOP = 12, 12, 4, 16
P_XBC = N_QKV
P_TURN = P_XBC + N_XBC
P_LOOP = P_TURN + N_TURN
P_WSSD = P_LOOP + N_LOOP
P_WGDN = P_WSSD + 8
P_WOUT = P_WGDN + 4
N_MIX = P_WOUT + 4
N_CONV = N_QKV + N_XBC

MOE_PIECES = 6 * EXPERTS
SSD_ORDER = [(0, 0), (1, 0), (0, 1), (1, 1), (2, 0), (2, 1), (3, 0), (3, 1)]
RING = 4
MOE_RING = 8
MOE_HI = 6
SCATTER_0, SCATTER_1, TURN_SEL, NEXT_GROUP = 3, 6, 10, 22

C_ID, C_STRICT, C_CAUSAL, C_IOTA, C_END = 0, 128, 256, 640, 768
Q_CONV, Q_BMERGE, Q_LN1, Q_SSDN, Q_GDNN, Q_END = 0, 240, 256, 264, 280, 281
R_BIAS, R_ALOG, R_D, R_BG, R_BE, R_END = 0, 40, 80, 112, 116, 132


def moe_order():
    order = []
    for e in range(EXPERTS + 1):
        if e < EXPERTS:
            order += [("gate", e, 0), ("gate", e, 1), ("up", e, 0), ("up", e, 1)]
        if e >= 1:
            order += [("down", e - 1, 0), ("down", e - 1, 1)]
    return order


ORDER = moe_order()
TURN_H = {ORDER.index(("up", e, 1)) + 2: e for e in range(EXPERTS)}


def hybrid_layer(nc, w_mix, w_small, w_router, w_gate, w_up, w_down, x, consts, masks, params, rows, ln2,
                 final_w, out):
    ctx = ExitStack()
    with ctx:
        def sem(name):
            return ctx.enter_context(nc.semaphore(name))

        def sb(name, shape, dt=F32):
            return ctx.enter_context(nc.sbuf_tensor(name, shape, dt))

        landing = ExitStack()
        raw = landing.enter_context(nc.sbuf_tensor("raw", [P, RING, PIECE], F32))
        landing.close()
        rawlo = sb("rawlo", [P, RING, PIECE], F32R)
        whi = sb("whi", [P, 2, PIECE], F32R)
        cst = sb("cst", [P, C_END])
        lmask = sb("lmask", [P, 2, LEVELS, P], U8)
        prm = sb("prm", [P, Q_END])
        row = sb("row", [P, R_END])
        strict_r = sb("strict_r", [P, P], F32R)
        ones_r = sb("ones_r", [P, P], F32R)
        stat = sb("stat", [P, 8, 32])
        stat_i = sb("stat_i", [P, 32], I32)
        act_r = sb("act_r", [P, 2, KC, SEQ], F32R)

        mixer = ExitStack()
        cv = mixer.enter_context(nc.sbuf_tensor("cv", [P, 48, SEQ], F32))
        xy = mixer.enter_context(nc.sbuf_tensor("xy", [P, NT, SSD_INNER], F32))
        gates = mixer.enter_context(nc.sbuf_tensor("gates", [P, 16, SEQ], F32))
        mixer.close()
        landing = ExitStack()
        moe_raw = landing.enter_context(nc.sbuf_tensor("moe_raw", [P, 4, PIECE], F32))
        landing.close()
        moe_lo = sb("moe_lo", [P, 4, PIECE], F32R)
        moe_hi = sb("moe_hi", [P, 2, PIECE], F32R)
        xy_r = sb("xy_r", [P, NT, SSD_INNER], F32R)
        gates_r = sb("gates_r", [P, 2, PIECE], F32R)
        z = cv[:, 24:40, :].rearrange("p a b -> p (a b)").rearrange("p (t c) -> p t c", t=NT)
        o = cv[:, 40:48, :].rearrange("p a b -> p (a b)").rearrange("p (t c) -> p t c", t=NT)
        kqt = cv[:, 0:16, :].rearrange("p a b -> p (a b)").rearrange("p (h c) -> p h c", h=GDN_HEADS)
        zg = kqt[:, 0:4, :].rearrange("p i (t c) -> p i t c", t=NT)
        sq = xy[:, :, :].rearrange("p t c -> p (t c)")
        allgates = gates[:, :, :].rearrange("p a b -> p (a b)")
        qn = allgates[:, 0:2048].rearrange("p (t c) -> p t c", t=NT)
        knorm1 = allgates[:, 2048:3072]
        spare = cv[:, 16:24, :].rearrange("p a b -> p (a b)")
        kq_h = spare[:, 0:1024]
        inv = spare[:, 1024:1536]
        invt = spare[:, 1536:2048]
        mask_in = cv[:, 40:47, :].rearrange("p a b -> p (a b)")
        merged = spare.rearrange("p (a b) -> p a b", a=KC)
        xin = xy[:, 0, :].rearrange("p (t c) -> p t c", t=NT)
        xn = xy[:, 1, :].rearrange("p (t c) -> p t c", t=NT)
        ht = xy_r[:, 1, :].rearrange("p (b i f s) -> p b i f s", b=2, i=2, f=4)
        u = xin
        fin_out = xin

        front = ExitStack()

        def fsb(name, shape, dt=F32):
            return front.enter_context(nc.sbuf_tensor(name, shape, dt))

        ktok = fsb("ktok", [P, GDN_DIM])
        vtok = fsb("vtok", [P, NT, GDN_DIM])
        cbt = fsb("cbt", [P, SSD_GROUPS, 384])
        dtv = fsb("dtv", [P, NT, DECAYS])
        vdec = fsb("vdec", [P, NT, DECAYS])
        vdec_h = fsb("vdec_h", [P, NT, DECAYS], F32R)
        vdec_l = fsb("vdec_l", [P, NT, DECAYS])
        beta = fsb("beta", [P, NT, GDN_HEADS])
        nbeta = fsb("nbeta", [P, NT, GDN_HEADS])
        egc = fsb("egc", [P, NT, GDN_HEADS])
        negc = fsb("negc", [P, GDN_HEADS])
        kdec = fsb("kdec", [P, GDN_HEADS])
        early = ExitStack()

        def esb(name, shape, dt=F32):
            return early.enter_context(nc.sbuf_tensor(name, shape, dt))

        small_sb = esb("small_sb", [P, NT, SMALL])
        tmp = esb("tmp", [P, 6, NT, DECAYS])
        heads16 = esb("heads16", [P, 31])
        ss16 = esb("ss16", [P, SEQ])
        cacc = esb("cacc", [P, 2, 2, SEQ])
        sml = esb("sml", [P, KC * SMALL])
        sml_h = esb("sml_h", [P, KC * SMALL], F32R)
        sml_l = esb("sml_l", [P, KC * SMALL], F32R)
        early.close()
        ssdrhs = fsb("ssdrhs", [P, 2, 2, 384], F32R)
        ldec = fsb("ldec", [P, 2, 384])
        gdnrhs = fsb("gdnrhs", [P, 2, 512], F32R)
        gdec = fsb("gdec", [P, 512])
        gdecm = fsb("gdecm", [P, 512])
        nmat = fsb("nmat", [P, 512])
        pmat = fsb("pmat", [P, 512])
        aqk = fsb("aqk", [P, 512])
        kq_t = fsb("kq_t", [P, 2, 256])
        kd = fsb("kd", [P, 2, P])
        vnew = fsb("vnew", [P, 2, 2, P])
        s1 = fsb("s1", [P, 256])
        resid = fsb("resid", [P, 2, P])
        qs = fsb("qs", [P, 256])
        sink = fsb("sink", [P, 16])
        xd = fsb("xd", [P, NT, 4, SSD_HD])
        front.close()

        hres = sb("hres", [P, NT, D])
        osq = hres[:, :, :].rearrange("p t c -> p (t c)")
        back = ExitStack()

        def bsb(name, shape, dt=F32):
            return back.enter_context(nc.sbuf_tensor(name, shape, dt))

        yt = bsb("yt", [P, 2, 16, SEQ], F32R)
        mtmp = bsb("mtmp", [P, 2, SEQ])
        rdiag = bsb("rdiag", [P, NT, P])
        orms = bsb("orms", [P, 16])
        rrow = bsb("rrow", [P, SEQ])
        back.close()

        mt_r = yt[:, :, 0:KC, :]
        zsq = z
        xg = sb("xg", [P, 2, KC, P], F32R)
        hs = sb("hs", [P, 2048])
        ut = hs[:, :].rearrange("p (k s) -> p k s", k=KC)
        hbuf = hs[:, 0:1024].rearrange("p (b f) -> p b f", b=2)
        sgate = hs[:, 1024:1536]
        ysp = sb("ysp", [P, 2, D], F32R)
        sel = sb("sel", [P, NT, P])
        selt = sb("selt", [P, NT, P], F32R)
        cslot = sb("cslot", [P, EXPERTS])
        ln2b = sb("ln2b", [P, D])
        finb = sb("finb", [P, D])
        wr = sb("wr", [P, KC * 20])
        rt = sb("rt", [P, 24, NT, 4])
        rl = sb("rl", [P, NT, 20])
        re = sb("re", [P, NT, 16])
        qsl = sb("qsl", [P, NT, 8])
        cw = sb("cw", [P, NT, EXPERTS])
        rinfo = sb("rinfo", [P, 8])
        rint = sb("rint", [P, 2], I32)
        mring = [raw[:, j, :] for j in range(RING)]
        mring += [moe_raw[:, j, :] for j in range(4)]
        los = [rawlo[:, j, :] for j in range(RING)] + [moe_lo[:, j, :] for j in range(4)]
        his = [t[:, j, :] for t in (whi, gates_r, moe_hi) for j in range(2)]
        back_his = [his[0], his[1], los[5]]
        assert len(mring) == MOE_RING and len(his) == MOE_HI

        ps = ctx.enter_context(nc.psum_tensor("ps", [P, 8, 512], F32))

        ident = cst[:, C_ID:C_ID + P]
        strict = cst[:, C_STRICT:C_STRICT + P]
        causal = cst[:, C_CAUSAL:C_CAUSAL + P]
        ones = cst[:, C_CAUSAL + P:C_CAUSAL + 2 * P]
        causal2 = cst[:, C_CAUSAL:C_CAUSAL + 256]
        causal3 = cst[:, C_CAUSAL:C_CAUSAL + 384]
        iota = cst[:, C_IOTA:C_IOTA + P]

        s_x, s_cst, s_tab, s_out = sem("s_x"), sem("s_cst"), sem("s_tab"), sem("s_out")
        s_sml, s_xres, s_moep, s_fin = sem("s_sml"), sem("s_xres"), sem("s_moep"), sem("s_fin")
        landed = [sem(f"landed{j}") for j in range(RING)]
        mlanded = [sem(f"mlanded{j}") for j in range(MOE_RING)]
        hi_done, lo_done, piece_mm = sem("hi_done"), sem("lo_done"), sem("piece_mm")
        acc_free = sem("acc_free")
        dve_step = sem("dve_step")
        ss_in, r_in, xn_done, xt_mm, xt_hi = (sem(n) for n in ("ss_in", "r_in", "xn_done", "xt_mm", "xt_hi"))
        xt_lo, cst_r, sml_hi, sml_lo, sml_mm = (sem(n) for n in ("xt_lo", "cst_r", "sml_hi", "sml_lo", "sml_mm"))
        tap3_done, tap_step, silu_done = sem("tap3_done"), sem("tap_step"), sem("silu_done")
        sq_done, ss_mm, norm_done = sem("sq_done"), sem("ss_mm"), sem("norm_done")
        fill_mm, evac_a, evac_d = sem("fill_mm"), sem("evac_a"), sem("evac_d")
        dec_in, dec_exp, dec_v, dec_mm, dec_tab, tab_done = (
            sem(n) for n in ("dec_in", "dec_exp", "dec_v", "dec_mm", "dec_tab", "tab_done"))
        g_staged, g_rhs, g_kq, g_seg, g_exp, g_mask, g_nt, g_aqk, g_kd, g_tail = (
            sem(n) for n in ("g_staged", "g_rhs", "g_kq", "g_seg", "g_exp", "g_mask", "g_nt", "g_aqk", "g_kd",
                             "g_tail"))
        g_eye, g_ntt, g_x, g_y, g_p, g_ps, g_xp, g_yp = (
            sem(n) for n in ("g_eye", "g_ntt", "g_x", "g_y", "g_p", "g_ps", "g_xp", "g_yp"))
        g_solve, g_vn, g_state, g_scopy, g_ocopy, g_ks, g_qs, g_r, g_o1, g_oadd = (
            sem(n) for n in ("g_solve", "g_vn", "g_state", "g_scopy", "g_ocopy", "g_ks", "g_qs", "g_r", "g_o1",
                             "g_oadd"))
        m_rhs, m_seg, m_exp, m_gl, m_y, m_xd, m_ydone = (
            sem(n) for n in ("m_rhs", "m_seg", "m_exp", "m_gl", "m_y", "m_xd", "m_ydone"))
        b_osq, b_red, b_o, b_z, b_yz, b_yss, b_yr, b_ys, b_gate, b_zg = (
            sem(n) for n in ("b_osq", "b_red", "b_o", "b_z", "b_yz", "b_yss", "b_yr", "b_ys", "b_gate", "b_zg"))
        bt_mm, bt_hi, bt_lo, b_m, b_mhi, b_mlo, b_h = (
            sem(n) for n in ("bt_mm", "bt_hi", "bt_lo", "b_m", "b_mhi", "b_mlo", "b_h"))
        b_mt, b_zs, b_rd = sem("b_mt"), sem("b_zs"), sem("b_rd")
        n_ss, n_u, n_ut, n_utc, n_log, n_lg, n_exp, n_cnt, n_route = (
            sem(n) for n in ("n_ss", "n_u", "n_ut", "n_utc", "n_log", "n_lg", "n_exp", "n_cnt",
                             "n_route"))
        e_sel, e_gath, e_xhi, e_xlo, e_silu, e_h, e_ht, e_hthi, e_htlo = (
            sem(n) for n in ("e_sel", "e_gath", "e_xhi", "e_xlo", "e_silu", "e_h", "e_ht", "e_hthi", "e_htlo"))
        e_cs = sem("e_cs")
        n_init, n_cw = sem("n_init"), sem("n_cw")
        e_turn, e_back, e_zero = sem("e_turn"), sem("e_back"), sem("e_zero")
        e_yhi, e_ylo, e_scat, e_add = (sem(n) for n in ("e_yhi", "e_ylo", "e_scat", "e_add"))
        f_ss, f_out = sem("f_ss"), sem("f_out")

        fills = [("v", i, "a") for i in range(4)] + [("x", i, "a") for i in range(8)]
        fills += [("k", i, "d") for i in range(4)] + [("cb", i, "d") for i in range(4)]
        fills += [("q", i, "d") for i in range(4)]
        fills += [("kqt", i, "a") for i in range(8)]
        fill_no, evac_no, seen = {}, [], {"a": 0, "d": 0}
        for f, (what, i, who) in enumerate(fills):
            fill_no[what, i] = f
            seen[who] += 1
            evac_no.append((who, seen[who]))

        def wait_evac(eng, f):
            who, n = evac_no[f]
            eng.wait_ge(evac_a if who == "a" else evac_d, n)

        def bank(f):
            return ps[:, 2 + f % 5, :]

        def f32(ap):
            return ap.bitcast(F32)

        def two(ap):
            return ap.rearrange("p (a b) -> p a b", a=2)

        def four(ap):
            return ap.rearrange("p (a b) -> p a b", a=4)

        back_bank = [4, 5, 6, 7, 4, 5, 6, 7, 6, 0, 1, 2, 3]
        SSD_BANKS = [0, 2, 4, 6]

        block = ctx.enter_context(nc.Block())

        @block.sync
        def _(sp):
            sp.dma_start(xin, x.rearrange("b (t p) c -> p (b t) c", p=P)).then_inc(s_x, 16)
            for p in range(RING):
                sp.dma_start(raw[:, p, :], w_mix[p]).then_inc(landed[p], 16)
            with sp.Fori(1, N_MIX // RING) as q:
                for j in range(RING):
                    sp.wait_ge(piece_mm, q * RING + (j - RING + 1))
                    sp.dma_start(raw[:, j, :], w_mix[bass.ds(q * RING + j, 1)].rearrange("a p c -> p (a c)"))\
                        .then_inc(landed[j], 16)

            def moe_piece(g, it, n, first):
                kind, e, half = ORDER[n]
                slot = n % MOE_RING
                if first and n < MOE_RING:
                    if slot < RING:
                        sp.wait_ge(piece_mm, N_MIX - RING + 1 + slot)
                    elif slot == RING + 1:
                        sp.wait_ge(piece_mm, N_MIX - 1)
                    elif slot == RING:
                        sp.wait_ge(b_mhi, 4)
                        sp.wait_ge(b_mlo, 4)
                else:
                    sp.wait_ge(piece_mm, it * MOE_PIECES + (N_MIX + n - MOE_RING + 1))
                w = {"gate": w_gate, "up": w_up, "down": w_down}[kind]
                src = w[bass.ds(g * EXPERTS + e, 1), :, half * PIECE:(half + 1) * PIECE]
                sp.dma_start(mring[slot], src.rearrange("a p c -> p (a c)")).then_inc(mlanded[slot], 16)

            for n in range(MOE_PIECES):
                moe_piece(0, 0, n, True)
            with sp.Fori(1, GROUPS) as g:
                for n in range(MOE_PIECES):
                    moe_piece(g, g, n, False)
            sp.wait_ge(n_route, 1)
            again = sp.value_load(rint[0:1, 0:1], min_val=GROUPS, max_val=GROUPS + 1)
            big = sp.value_load(rint[0:1, 1:2], min_val=0, max_val=GROUPS - 1)
            with sp.If(again > GROUPS):
                for n in range(MOE_PIECES):
                    moe_piece(big, GROUPS, n, False)
            for t in range(NT):
                sp.wait_ge(f_out, t + 1)
                sp.dma_start(out[0, t * P:(t + 1) * P, :], fin_out[:, t, :]).then_inc(s_out, 16)
            sp.wait_ge(s_out, 16 * NT)

        @block.scalar
        def _(act):
            act.dma_start(cst[:, :], consts).then_inc(s_cst, 16)
            act.dma_start(prm[:, :], params).then_inc(s_cst, 16)
            act.dma_start(sml[:, :], w_small).then_inc(s_sml, 16)
            act.dma_start(row[:, :], rows.partition_broadcast(P)).then_inc(s_tab, 16)
            act.dma_start(mask_in, masks).then_inc(s_tab, 16)

            def mix_hi(p):
                act.wait_ge(landed[p % RING], p // RING * 16 + 16)
                if p >= P_WSSD + 3:
                    act.wait_ge(piece_mm, p - 2)
                act.copy(back_his[(p - P_WSSD) % 3], raw[:, p % RING, :]).then_inc(hi_done, 1)

            def hi(q, j, slots=2):
                act.wait_ge(landed[j], q * 16 + 16)
                if not (isinstance(q, int) and q == 0):
                    act.wait_ge(piece_mm, q * RING + (j - slots + 1))
                act.copy(his[j % slots], raw[:, j, :]).then_inc(hi_done, 1)

            act.wait_ge(s_x, 16)
            for t in range(NT):
                act.activation(xn[:, t, :], xin[:, t, :], ACT.Square,
                               accum_out=stat[:, 0, t:t + 1]).then_inc(ss_in, 1)
            act.wait_ge(r_in, 1)
            act.wait_ge(ss_in, NT)
            for t in range(NT):
                act.activation(xn[:, t, :], xin[:, t, :], ACT.Copy,
                               scale=stat[:, 1, t:t + 1]).then_inc(xn_done, 1)
            hi(0, 0)
            act.wait_ge(s_cst, 32)
            for k in range(KC):
                act.wait_ge(xt_mm, k // 2 + 1)
                act.activation(act_r[:, 0, k, :], ps[:, 2 + k // 2, (k % 2) * SEQ:(k % 2 + 1) * SEQ], ACT.Copy,
                               scale=prm[:, Q_LN1 + k:Q_LN1 + k + 1]).then_inc(xt_hi, 1)
            hi(0, 1)
            act.wait_ge(s_sml, 16)
            act.copy(sml_h[:, :], sml[:, :]).then_inc(sml_hi, 1)

            def tap3(p, j):
                act.wait_ge(piece_mm, p + 1)
                if isinstance(p, int) and p < 2:
                    pass
                else:
                    act.wait_ge(silu_done, p - 1)
                for m in range(2):
                    c = Q_CONV + m * 5
                    ins = act.activation(cacc[:, j % 2, m, :], ps[:, j, m * SEQ:(m + 1) * SEQ], ACT.Identity,
                                         bias=prm[:, bass.ds(p * 10 + (c + 4), 1)],
                                         scale=prm[:, bass.ds(p * 10 + (c + 3), 1)])
                ins.then_inc(tap3_done, 1)

            def silu(p, j):
                act.wait_ge(tap_step, p * 6 + 6)
                act.activation(cv[:, bass.ds(p * 2, 2), :], cacc[:, j % 2, :, :], ACT.Silu).then_inc(silu_done, 1)

            act.wait_ge(cst_r, 3)
            for p in range(RING):
                hi((p + 2) // RING, (p + 2) % RING, RING)
                tap3(p, p)
                if p >= 1:
                    silu(p - 1, p - 1)
                if p == 2:
                    act.wait_ge(dec_in, 1)
                    act.wait_ge(s_tab, 32)
                    act.activation(tmp[:, 2, :, :], tmp[:, 1, :, :], ACT.Exp).then_inc(dec_exp, 1)
                    act.activation(tmp[:, 4, 0, :], row[:, R_ALOG:R_ALOG + DECAYS], ACT.Exp).then_inc(dec_exp, 1)
                    act.activation(beta[:, :, :], nbeta[:, :, :], ACT.Exp).then_inc(dec_exp, 1)
            with act.Fori(1, N_CONV // RING) as q:
                for j in range(RING):
                    hi(q + (j + 2) // RING, (j + 2) % RING, RING)
                    tap3(q * RING + j, j)
                    silu(q * RING + (j - 1), j - 1)
            silu(N_CONV - 1, 1)

            act.wait_ge(dec_mm, 1)
            act.activation(egc[:, :, :], ps[:, 6, 0:16].rearrange("p (t h) -> p t h", t=NT),
                           ACT.Exp).then_inc(dec_tab, 1)
            act.activation(kdec[:, :], ps[:, 6, 16:24], ACT.Exp).then_inc(dec_tab, 1)
            def evac(what, i, dst):
                f = fill_no[what, i]
                act.wait_ge(fill_mm, f + 1)
                act.copy(dst, bank(f)).then_inc(evac_a, 1)

            def z_silu(i):
                act.wait_ge(piece_mm, P_TURN + i + 1)
                act.activation(z[:, :, i * COLS:(i + 1) * COLS], two(ps[:, i % 2, :]), ACT.Silu).then_inc(acc_free, 1)

            act.wait_ge(ss_mm, 1)
            for i in range(4):
                evac("v", i, vtok[:, i % NT, (i // NT) * 512:(i // NT + 1) * 512])
            hi(*divmod(P_TURN + 2, RING))
            for i in range(8):
                evac("x", i, xy[:, i % NT, (i // NT) * 512:(i // NT + 1) * 512])
            z_silu(0)
            z_silu(1)
            hi(*divmod(P_TURN + 3, RING))
            z_silu(2)
            hi(*divmod(P_TURN + 4, RING))
            for i in range(GDN_HEADS):
                evac("kqt", i, kqt[:, i, :])
            z_silu(3)
            hi(*divmod(P_TURN + 5, RING))

            with act.Fori(0, GDN_HEADS // 2) as it:
                def take(j):
                    act.wait_ge(piece_mm, it * 4 + (P_LOOP + j + 1))
                    if j == 0:
                        act.copy(z[:, :, bass.ds(it * COLS + N_TURN * COLS, COLS)],
                                 two(ps[:, 0, :])).then_inc(acc_free, 1)
                    elif j == 2:
                        act.copy(zg[:, bass.ds(it, 1), :, :].rearrange("p i t c -> p (i t) c"),
                                 two(ps[:, 0, :])).then_inc(acc_free, 1)
                    else:
                        for m in range(2):
                            ins = act.activation(
                                gates[:, bass.ds(it * 4 + ((j // 2) * 2 + m), 1), :].rearrange("p a b -> p (a b)"),
                                ps[:, 1, m * SEQ:(m + 1) * SEQ], ACT.Identity,
                                bias=prm[:, bass.ds(it * 4 + (Q_BMERGE + (j // 2) * 2 + m), 1)])
                        ins.then_inc(acc_free, 1)

                def decay_exp(k):
                    act.wait_ge(m_seg, it * 8 + (k + 1))
                    if k >= 2:
                        act.wait_ge(m_y, it * 8 + (k - 1))
                    act.activation(ldec[:, k % 2, :], ps[:, 5 + k % 2, 0:384], ACT.Exp).then_inc(m_exp, 1)

                def pcopy(l):
                    act.wait_ge(g_p, it * 6 + l)
                    act.copy(pmat[:, :], ps[:, 2, :]).then_inc(g_ps, 1)

                def xcopy(l):
                    act.wait_ge(g_xp, it * 5 + l)
                    act.copy(inv, ps[:, 3, :]).then_inc(g_x, 1)

                def vscale(c):
                    act.wait_ge(g_solve, it * 2 + (c + 1))
                    for h in range(2):
                        ins = act.activation(vnew[:, c, h, :], ps[:, 2, h * P:(h + 1) * P], ACT.Copy,
                                             scale=beta[:, c, bass.ds(it * 2 + h, 1)])
                    ins.then_inc(g_vn, 1)

                for h in range(2):
                    ins = act.activation(kd[:, h, :], ktok[:, bass.ds(it * 256 + h * P, P)], ACT.Copy,
                                         scale=kdec[:, bass.ds(it * 2 + h, 1)])
                ins.then_inc(g_kd, 1)
                act.wait_ge(g_seg, it + 1)
                act.activation(gdec[:, :], ps[:, 4, :], ACT.Exp).then_inc(g_exp, 1)
                decay_exp(0)
                decay_exp(1)
                pcopy(1)
                decay_exp(2)
                decay_exp(3)
                xcopy(1)
                pcopy(2)
                take(0)
                decay_exp(4)
                hi(it + P_LOOP // RING, 2)
                decay_exp(5)
                xcopy(2)
                pcopy(3)
                decay_exp(6)
                decay_exp(7)
                xcopy(3)
                pcopy(4)
                take(1)
                hi(it + P_LOOP // RING, 3)
                xcopy(4)
                pcopy(5)
                xcopy(5)
                pcopy(6)
                vscale(0)
                act.wait_ge(g_state, it + 1)
                act.copy(s1[:, :], ps[:, 3, 0:256]).then_inc(g_scopy, 1)
                take(2)
                hi(it + (P_LOOP // RING + 1), 0)
                act.wait_ge(g_ks, it + 1)
                for h in range(2):
                    ins = act.activation(qs[:, h * P:(h + 1) * P], ps[:, 3, h * P:(h + 1) * P], ACT.Copy,
                                         scale=egc[:, 1, bass.ds(it * 2 + h, 1)])
                ins.then_inc(g_qs, 1)
                vscale(1)
                take(3)
                hi(it + (P_LOOP // RING + 1), 1)

            def back_hi(f):
                act.wait_ge(bt_mm, f + 1)
                if f > 8:
                    i = f - 9
                    act.activation(act_r[:, 0, 2 * i:2 * i + 2, :], two(ps[:, back_bank[f], :]), ACT.Copy,
                                   scale=prm[:, Q_GDNN:Q_GDNN + 1]).then_inc(bt_hi, 1)
                else:
                    for m in range(2):
                        a = 2 * f + m
                        ins = act.activation(yt[:, 0, a, :], ps[:, back_bank[f], m * SEQ:(m + 1) * SEQ], ACT.Copy,
                                             scale=prm[:, Q_SSDN + a:Q_SSDN + a + 1])
                    ins.then_inc(bt_hi, 1)

            act.wait_ge(g_oadd, GDN_HEADS // 2 + 1)
            for f in range(4):
                back_hi(f)
            for t in range(NT):
                act.activation(z[:, t, 1024:2048], z[:, t, 1024:2048], ACT.Silu).then_inc(b_z, 1)
            mix_hi(P_WSSD + 2)
            act.activation(osq, o.rearrange("p t c -> p (t c)"), ACT.Square).then_inc(b_osq, 1)
            for f in range(4, 8):
                back_hi(f)
            mix_hi(P_WSSD + 3)
            for h in range(2):
                for t in range(NT):
                    act.wait_ge(b_yz, NT * h + t + 1)
                    act.activation(zsq[:, t, h * 1024:(h + 1) * 1024], xy[:, t, h * 1024:(h + 1) * 1024], ACT.Square,
                                   accum_out=stat[:, 5, 2 * t + h:2 * t + h + 1]).then_inc(b_yss, 1)
            act.activation(zg, zg, ACT.Silu).then_inc(b_zs, 1)
            for i in range(4):
                gi = gates[:, 4 * i:4 * i + 4, :].rearrange("p a b -> p (a b)")
                act.activation(gi, gi, ACT.Tanh, scale=0.5).then_inc(b_gate, 1)
            mix_hi(P_WSSD + 4)
            act.wait_ge(b_red, 1)
            act.dma_start(hres[:, :, :], x.rearrange("b (t p) c -> p (b t) c", p=P)).then_inc(s_xres, 16)
            mix_hi(P_WSSD + 5)
            mix_hi(P_WSSD + 6)
            mix_hi(P_WSSD + 7)
            for f in range(9, 13):
                back_hi(f)
            for p in range(P_WGDN, P_WGDN + 3):
                mix_hi(p)
            for i in range(4):
                mix_hi(P_WGDN + 3 + i)
                act.wait_ge(b_m, 5 + i)
                act.copy(mt_r[:, 0, 2 * i:2 * i + 2, :], merged[:, 2 * i:2 * i + 2, :]).then_inc(b_mhi, 1)
                if i == 0:
                    act.dma_start(ln2b[:, :], ln2.partition_broadcast(P)).then_inc(s_moep, 16)
                    act.dma_start(wr[:, :], w_router).then_inc(s_moep, 16)
            mix_hi(N_MIX - 1)

            act.dma_start(finb[:, :], final_w.partition_broadcast(P)).then_inc(s_fin, 16)
            for i in range(4):
                act.wait_ge(n_ut, i + 1)
                act.copy(ut[:, 2 * i:2 * i + 2, :], two(ps[:, i % 2, :])).then_inc(n_utc, 1)
                act.wait_ge(b_h, i + 1)
                for t in range(NT):
                    act.activation(act_r[:, t, 2 * i, :], hres[:, t, i * COLS:(i + 1) * COLS], ACT.Square,
                                   accum_out=stat[:, 5, i * NT + t:i * NT + t + 1]).then_inc(n_ss, 1)
            act.wait_ge(n_lg, 1)
            act.activation(rt[:, 4, :, :], rt[:, 3, :, :], ACT.Exp).then_inc(n_exp, 1)
            act.wait_ge(n_lg, 2)
            act.activation(rt[:, 16, :, 0:1], rt[:, 15, :, 0:1], ACT.Exp).then_inc(n_exp, 1)
            act.wait_ge(n_route, 1)
            runs = act.value_load(rint[0:1, 0:1], min_val=GROUPS, max_val=GROUPS + 1)

            def x_high(it):
                act.wait_ge(e_gath, it + 1)
                act.copy(xg[:, 0, :, :].rearrange("p k s -> p (k s)"),
                         ps[:, 0:2, :].rearrange("p a b -> p (a b)")).then_inc(e_xhi, 1)

            def y_high(it):
                act.wait_ge(e_zero, 2)
                act.wait_ge(piece_mm, it * MOE_PIECES + N_MIX)
                act.copy(ysp[:, 0, :], ps[:, 4:6, :].rearrange("p a b -> p (a b)")).then_inc(e_yhi, 1)

            with act.Fori(0, runs) as it:
                def mhi(n):
                    slot = n % MOE_RING
                    act.wait_ge(mlanded[slot], it * (16 * MOE_PIECES // MOE_RING) + 16 * (n // MOE_RING + 1))
                    act.wait_ge(piece_mm, it * MOE_PIECES + (N_MIX + n - MOE_HI + 1))
                    act.copy(his[n % MOE_HI], mring[slot]).then_inc(hi_done, 1)

                mhi(0)
                x_high(it)
                mhi(1)
                y_high(it)
                mhi(2)
                mhi(3)
                for n, (kind, e, half) in enumerate(ORDER):
                    if n + 4 < MOE_PIECES:
                        mhi(n + 4)
                    if (kind, half) == ("gate", 1):
                        act.wait_ge(piece_mm, it * MOE_PIECES + (N_MIX + n + 1))
                        if e >= 1:
                            act.wait_ge(e_h, it * EXPERTS + e)
                        act.activation(sgate, ps[:, 2 * (e % 2), :], ACT.Silu).then_inc(e_silu, 1)
                    if n + 1 in TURN_H:
                        d = TURN_H[n + 1]
                        act.wait_ge(e_ht, it * EXPERTS + (d + 1))
                        act.copy(ht[:, d % 2, 0, :, :].rearrange("p a b -> p (a b)"), ps[:, 6, :]).then_inc(e_hthi, 1)
                    if n + 1 == TURN_SEL:
                        act.wait_ge(e_turn, it + 1)
                        act.copy(selt[:, :, :].rearrange("p t s -> p (t s)"), ps[:, 7, P:3 * P]).then_inc(e_back, 1)
            y_high(runs)

            act.wait_ge(e_add, runs * 2 + 2)
            for t in range(NT):
                act.activation(u[:, t, :], hres[:, t, :], ACT.Square, accum_out=stat[:, 0, t:t + 1]).then_inc(f_ss, 1)

        @block.vector
        def _(dve):
            chain = [0]

            def link(ins):
                chain[0] += 1
                ins.then_inc(dve_step, 1)
                dve.wait_ge(dve_step, chain[0])

            def rsqrt(n, scale, last_sem):
                v, y, t1, t2 = (stat[:, i, 0:n] for i in (2, 1, 3, 4))
                link(dve.tensor_scalar(v, stat[:, 0, 0:n], scale, EPS, ALU.mult, ALU.add))
                link(dve.tensor_scalar(stat_i[:, 0:n], v.bitcast(I32), 1, None, ALU.logical_shift_right))
                link(dve.tensor_scalar(y.bitcast(I32), stat_i[:, 0:n], -1.0, 1597463007.0, ALU.mult, ALU.add))
                for i in range(4):
                    link(dve.scalar_tensor_tensor(t1, y, -0.5, y, ALU.mult, ALU.mult))
                    link(dve.tensor_tensor(t2, t1, v, ALU.mult))
                    ins = dve.scalar_tensor_tensor(y, t2, 1.5, y, ALU.add, ALU.mult)
                    if i < 3 or last_sem is None:
                        link(ins)
                    else:
                        ins.then_inc(last_sem, 1)

            def lo(q, j, slots=2):
                dve.wait_ge(hi_done, q * RING + (j + 1))
                dve.tensor_tensor(los[j], raw[:, j, :], f32(his[j % slots]),
                                  ALU.subtract).then_inc(lo_done, 1)

            dve.wait_ge(ss_in, NT)
            rsqrt(NT, 1.0 / D, r_in)
            lo(0, 0)
            dve.wait_ge(s_cst, 32)
            for k in range(KC):
                dve.wait_ge(xt_hi, k // 2 * 2 + 2)
                dve.scalar_tensor_tensor(act_r[:, 1, k, :], ps[:, 2 + k // 2, (k % 2) * SEQ:(k % 2 + 1) * SEQ],
                                         prm[:, Q_LN1 + k:Q_LN1 + k + 1], f32(act_r[:, 0, k, :]),
                                         ALU.mult, ALU.subtract).then_inc(xt_lo, 1)
            lo(0, 1)
            dve.wait_ge(sml_hi, 1)
            dve.tensor_tensor(sml_l[:, :], sml[:, :], f32(sml_h[:, :]), ALU.subtract).then_inc(sml_lo, 1)
            dve.tensor_copy(strict_r[:, :], strict).then_inc(cst_r, 1)
            dve.tensor_copy(ones_r[:, :], ones).then_inc(cst_r, 1)
            dve.wait_ge(s_tab, 32)
            dve.tensor_copy(lmask[:, :, :, :].rearrange("p a l c -> p (a l c)"),
                            mask_in).then_inc(cst_r, 1)

            def taps(p, j):
                dve.wait_ge(tap3_done, p + 1)
                for k in (1, 2, 3):
                    for m in range(2):
                        if k >= 2:
                            dve.wait_ge(tap_step, p * 6 + (2 * (k - 2) + m + 1))
                        acc = cacc[:, j % 2, m, k:SEQ]
                        dve.scalar_tensor_tensor(acc, ps[:, j, m * SEQ:(m + 1) * SEQ - k],
                                                 prm[:, bass.ds(p * 10 + (Q_CONV + m * 5 + 3 - k), 1)], acc,
                                                 ALU.mult, ALU.add).then_inc(tap_step, 1)

            pre, na, e, s2, acc, s = (tmp[:, i, :, :] for i in (0, 1, 2, 3, 4, 5))

            def decays_in():
                dve.wait_ge(sml_mm, 1)
                link(dve.tensor_copy(small_sb[:, :, :],
                                     ps[:, 6, 0:NT * SMALL].rearrange("p (t c) -> p t c", t=NT)))
                link(dve.tensor_tensor(pre, small_sb[:, :, 0:DECAYS],
                                       row[:, R_BIAS:R_BIAS + DECAYS].unsqueeze(1).broadcast_to([P, NT, DECAYS]), ALU.add))
                link(dve.tensor_scalar(na, pre, -1.0, None, ALU.mult))
                link(dve.tensor_tensor(na, na, pre, ALU.min))
                dve.tensor_scalar(nbeta[:, :, :], small_sb[:, :, DECAYS:SMALL], -1.0, 80.0,
                                  ALU.mult, ALU.min).then_inc(dec_in, 1)

            def decays_out():
                dve.wait_ge(dec_exp, 3)
                a_neg = stat[:, 5:7, :].rearrange("p a b -> p (a b)")[:, 0:DECAYS]
                link(dve.tensor_scalar(a_neg, tmp[:, 4, 0, :], -1.0, None, ALU.mult))
                link(dve.tensor_scalar(acc, e, 2.0, None, ALU.add))
                link(dve.reciprocal(s2, acc))
                link(dve.tensor_tensor(s, e, s2, ALU.mult))
                link(dve.tensor_tensor(s2, s, s, ALU.mult))
                link(dve.tensor_scalar(acc, s2, 1.0 / 15, None, ALU.mult))
                for c in (13, 11, 9, 7, 5, 3):
                    link(dve.scalar_tensor_tensor(acc, acc, 1.0 / c, s2, ALU.add, ALU.mult))
                link(dve.scalar_tensor_tensor(acc, acc, 1.0, s, ALU.add, ALU.mult))
                link(dve.tensor_scalar(na, pre, 0.0, None, ALU.max))
                link(dve.scalar_tensor_tensor(dtv[:, :, :], acc, 2.0, na, ALU.mult, ALU.add))
                link(dve.tensor_tensor(vdec[:, :, :], dtv[:, :, :],
                                       a_neg.unsqueeze(1).broadcast_to([P, NT, DECAYS]), ALU.mult))
                link(dve.tensor_copy(vdec_h[:, :, :], vdec[:, :, :]))
                dve.tensor_tensor(vdec_l[:, :, :], vdec[:, :, :], f32(vdec_h[:, :, :]), ALU.subtract).then_inc(dec_v, 1)
                link(dve.tensor_scalar(beta[:, :, :], beta[:, :, :], 1.0, None, ALU.add))
                link(dve.reciprocal(beta[:, :, :], beta[:, :, :]))
                dve.tensor_scalar(nbeta[:, :, :], beta[:, :, :], -1.0, None, ALU.mult).then_inc(tab_done, 1)

            for p in range(RING):
                lo((p + 2) // RING, (p + 2) % RING, RING)
                taps(p, p)
                if p == 1:
                    decays_in()
            decays_out()
            with dve.Fori(1, N_CONV // RING) as q:
                for j in range(RING):
                    lo(q + (j + 2) // RING, (j + 2) % RING, RING)
                    taps(q * RING + j, j)
            dve.wait_ge(ss_mm, 1)
            dve.tensor_copy(ss16[0:16, :], ps[0:16, 7, 0:SEQ]).then_inc(ss_mm, 1)
            dve.wait_ge(dec_tab, 2)
            dve.tensor_scalar(negc[:, :], egc[:, 1, :], -1.0, None, ALU.mult).then_inc(tab_done, 1)
            dve.wait_ge(tap_step, 6 * N_CONV)
            dve.memset(stat[:, 7, 0:1], 0.0).then_inc(acc_free, 2)

            dve.wait_ge(ss_mm, 3)
            link(dve.tensor_copy(stat[:, 0, :], ps[:, 7, 0:32]))
            rsqrt(32, 1.0, None)
            rq = stat[:, 1, :].rearrange("p (t h) -> p t h", t=NT)
            link(dve.tensor_scalar(rq[:, :, 0:8], rq[:, :, 0:8], float(P) ** -0.5, None, ALU.mult))

            def norm_evac(what, off):
                for i in range(4):
                    f = fill_no[what, i]
                    t, b = i % NT, i // NT
                    dst = qn[:, t, :] if what == "q" else (ktok[:, :] if t == 0 else knorm1)
                    dve.wait_ge(fill_mm, f + 1)
                    dve.tensor_tensor(
                        four(dst[:, b * 512:(b + 1) * 512]), four(bank(f)),
                        rq[:, t, off + 4 * b:off + 4 * b + 4].unsqueeze(2).broadcast_to([P, 4, P]),
                        ALU.mult).then_inc(evac_d, 1)

            norm_evac("k", 8)
            lo(*divmod(P_TURN + 2, RING))
            for i in range(SSD_GROUPS):
                f = fill_no["cb", i]
                dve.wait_ge(fill_mm, f + 1)
                dve.tensor_tensor(cbt[:, i, :], bank(f)[:, 0:384], causal3, ALU.mult).then_inc(evac_d, 1)
            norm_evac("q", 0)
            dve.memset(sink[:, 15:16], 0.0).then_inc(g_oadd, 1)
            for i in (3, 4, 5):
                lo(*divmod(P_TURN + i, RING))

            with dve.Fori(0, GDN_HEADS // 2) as it:
                def scores(k):
                    dve.wait_ge(m_exp, it * 8 + (k + 1))
                    for t, (a, b) in enumerate(((0, 256), (256, 384))):
                        ins = dve.scalar_tensor_tensor(
                            ldec[:, k % 2, a:b], cbt[:, bass.ds(it, 1), a:b].rearrange("p a b -> p (a b)"),
                            dtv[:, t, bass.ds(it * 8 + k, 1)], ldec[:, k % 2, a:b], ALU.mult, ALU.mult)
                    ins.then_inc(m_gl, 1)

                def merge_level(l):
                    dve.wait_ge(g_yp, it * 6 + l)
                    dve.wait_ge(g_y, it * 7 + l)
                    dve.memset(sink[:, 2 * l + 1:2 * l + 2], 0.0)
                    dve.copy_predicated(four(invt), lmask[:, 1, l, :].unsqueeze(1).broadcast_to([P, 4, P]),
                                        four(ps[:, 4, :])).then_inc(g_y, 1)

                def y_add(k):
                    dve.wait_ge(m_y, it * 8 + (4 * k + 4))
                    dve.wait_ge(m_xd, it * 2 + (k + 1))
                    dve.tensor_tensor(xy[:, :, bass.ds(it * 512 + k * 256, 256)], two(ps[:, 7, :]),
                                      xd[:, :, :, :].rearrange("p t h d -> p t (h d)"), ALU.add).then_inc(m_ydone, 1)

                dve.wait_ge(g_kq, it + 1)
                dve.wait_ge(g_exp, it + 1)
                for h in range(2):
                    for c in range(NT):
                        n = 2 * h + c
                        ins = dve.scalar_tensor_tensor(
                            nmat[:, n * P:(n + 1) * P], ps[:, 2 + h, c * 256:c * 256 + P],
                            nbeta[:, c, bass.ds(it * 2 + h, 1)], gdec[:, n * P:(n + 1) * P], ALU.mult, ALU.mult)
                ins.then_inc(g_nt, 1)
                scores(0)
                scores(1)
                dve.wait_ge(g_mask, it + 1)
                for h in range(2):
                    ins = dve.tensor_tensor(two(aqk[:, h * 256:(h + 1) * 256]), two(ps[:, 2 + h, :])[:, :, P:2 * P],
                                            two(gdecm[:, h * 256:(h + 1) * 256]), ALU.mult)
                ins.then_inc(g_aqk, 1)
                dve.wait_ge(g_eye, it * 2 + 2)
                dve.wait_ge(g_ntt, it + 1)
                dve.wait_ge(g_nt, it + 1)
                dve.memset(sink[:, 0:1], 0.0)
                dve.copy_predicated(four(inv), lmask[:, 0, 0, :].unsqueeze(1).broadcast_to([P, 4, P]),
                                    four(ps[:, 4, :])).then_inc(g_x, 1)
                dve.copy_predicated(four(invt), lmask[:, 1, 0, :].unsqueeze(1).broadcast_to([P, 4, P]),
                                    four(nmat[:, :])).then_inc(g_y, 1)
                merge_level(1)
                scores(2)
                scores(3)
                merge_level(2)
                y_add(0)
                scores(4)
                lo(it + P_LOOP // RING, 2)
                scores(5)
                merge_level(3)
                scores(6)
                scores(7)
                merge_level(4)
                lo(it + P_LOOP // RING, 3)
                y_add(1)
                merge_level(5)
                merge_level(6)
                dve.wait_ge(g_state, it + 1)
                dve.tensor_copy(o[:, 0, bass.ds(it * 256, 256)], ps[:, 4, 0:256]).then_inc(g_ocopy, 1)
                dve.wait_ge(g_ks, it + 1)
                for h in range(2):
                    ins = dve.scalar_tensor_tensor(resid[:, h, :], ps[:, 2, h * P:(h + 1) * P],
                                                   negc[:, bass.ds(it * 2 + h, 1)],
                                                   vtok[:, 1, bass.ds(it * 256 + h * P, P)], ALU.mult, ALU.add)
                ins.then_inc(g_r, 1)
                lo(it + (P_LOOP // RING + 1), 0)
                dve.wait_ge(g_o1, it + 1)
                dve.wait_ge(g_qs, it + 1)
                dve.tensor_tensor(o[:, 1, bass.ds(it * 256, 256)], ps[:, 4, 0:256], qs[:, :],
                                  ALU.add).then_inc(g_oadd, 1)
                lo(it + (P_LOOP // RING + 1), 1)

            def back_lo(f):
                if f == 8:
                    dve.wait_ge(bt_mm, f + 1)
                    dve.tensor_copy(rrow[:, :], ps[:, back_bank[f], 0:SEQ]).then_inc(bt_lo, 1)
                    return
                dve.wait_ge(bt_hi, f + (f < 8))
                if f > 8:
                    i = f - 9
                    dve.scalar_tensor_tensor(act_r[:, 1, 2 * i:2 * i + 2, :].rearrange("p a b -> p (a b)"),
                                             ps[:, back_bank[f], :], prm[:, Q_GDNN:Q_GDNN + 1],
                                             f32(act_r[:, 0, 2 * i:2 * i + 2, :].rearrange("p a b -> p (a b)")),
                                             ALU.mult, ALU.subtract).then_inc(bt_lo, 1)
                else:
                    for m in range(2):
                        a = 2 * f + m
                        ins = dve.scalar_tensor_tensor(yt[:, 1, a, :], ps[:, back_bank[f], m * SEQ:(m + 1) * SEQ],
                                                       prm[:, Q_SSDN + a:Q_SSDN + a + 1], f32(yt[:, 0, a, :]),
                                                       ALU.mult, ALU.subtract)
                    ins.then_inc(bt_lo, 1)

            def mix_lo(p):
                dve.wait_ge(hi_done, p + 1)
                dve.tensor_tensor(los[p % RING], raw[:, p % RING, :], f32(back_his[(p - P_WSSD) % 3]),
                                  ALU.subtract).then_inc(lo_done, 1)

            def gate_y(t, h):
                c = slice(h * 1024, (h + 1) * 1024)
                dve.tensor_tensor(xy[:, t, c], xy[:, t, c], z[:, t, c], ALU.mult).then_inc(b_yz, 1)

            for f in range(4):
                back_lo(f)
            for t in range(NT):
                dve.wait_ge(b_z, t + 1)
                dve.wait_ge(b_yz, NT)
                gate_y(t, 1)
            mix_lo(P_WSSD + 2)
            for f in range(4, 8):
                back_lo(f)
            dve.wait_ge(b_osq, 1)
            link(dve.tensor_reduce(stat[:, 0, 0:16], osq.rearrange("p (n d) -> p n d", d=P), AX_X, ALU.add))
            rsqrt(16, 1.0 / P, None)
            dve.tensor_copy(orms[:, :], stat[:, 1, 0:16]).then_inc(b_red, 1)
            mix_lo(P_WSSD + 3)
            dve.wait_ge(b_yss, 2 * NT)
            dve.wait_ge(b_red, 1)
            link(dve.tensor_tensor(stat[:, 0, 0:NT], stat[:, 5, 0:2 * NT:2], stat[:, 5, 1:2 * NT:2], ALU.add))
            rsqrt(NT, 1.0 / SSD_INNER, None)
            for t in range(NT):
                dve.tensor_scalar(rdiag[:, t, :], ident, stat[:, 1, t:t + 1], None, ALU.mult).then_inc(b_rd, 1)
            dve.wait_ge(b_gate, 4)
            dve.tensor_scalar(allgates, allgates, 0.5, 0.5, ALU.mult, ALU.add).then_inc(b_zg, 1)
            mix_lo(P_WSSD + 4)
            back_lo(8)
            dve.wait_ge(b_zg, 1)
            dve.wait_ge(bt_lo, 9)
            dve.tensor_tensor(gates[:, 0:8, :], gates[:, 0:8, :],
                              rrow[:, :].unsqueeze(1).broadcast_to([P, 8, SEQ]), ALU.mult).then_inc(b_zg, 1)
            dve.wait_ge(b_zg, 2)

            def merge_ssd(cb):
                dve.wait_ge(piece_mm, P_WSSD + SSD_ORDER.index((cb, 1)) + 1)
                dve.tensor_tensor(merged[:, 2 * cb:2 * cb + 2, :], gates[:, 2 * cb:2 * cb + 2, :],
                                  ps[:, SSD_BANKS[cb]:SSD_BANKS[cb] + 2, 0:SEQ], ALU.mult).then_inc(b_m, 1)

            def merge_gdn(i):
                dve.wait_ge(piece_mm, P_WGDN + i + 1)
                if i >= 1:
                    dve.wait_ge(b_m, 4 + i)
                dve.tensor_tensor(mtmp[:, :, :], gates[:, 8 + 2 * i:10 + 2 * i, :],
                                  two(ps[:, i, :]), ALU.mult).then_inc(b_mt, 1)
                dve.wait_ge(b_mt, i + 1)
                dve.wait_ge(b_m, 4)
                dve.tensor_tensor(merged[:, 2 * i:2 * i + 2, :], merged[:, 2 * i:2 * i + 2, :],
                                  mtmp[:, :, :], ALU.add).then_inc(b_m, 1)

            def merged_lo(i):
                dve.wait_ge(b_mhi, i + 1)
                dve.wait_ge(b_m, 5 + i)
                dve.tensor_tensor(mt_r[:, 1, 2 * i:2 * i + 2, :], merged[:, 2 * i:2 * i + 2, :],
                                  f32(mt_r[:, 0, 2 * i:2 * i + 2, :]), ALU.subtract).then_inc(b_mlo, 1)

            merge_ssd(0)
            mix_lo(P_WSSD + 5)
            merge_ssd(1)
            mix_lo(P_WSSD + 6)
            mix_lo(P_WSSD + 7)
            for f in range(9, 13):
                back_lo(f)
            mix_lo(P_WGDN)
            merge_ssd(2)
            mix_lo(P_WGDN + 1)
            mix_lo(P_WGDN + 2)
            merge_ssd(3)
            for i in range(4):
                merge_gdn(i)
                mix_lo(P_WGDN + 3 + i)
                merged_lo(i)
            mix_lo(N_MIX - 1)
            dve.wait_ge(s_xres, 16)
            dve.wait_ge(s_moep, 32)
            for i in range(4):
                p = P_WOUT + i
                cols = slice(i * COLS, (i + 1) * COLS)
                dve.wait_ge(piece_mm, p + 1)
                dve.tensor_tensor(hres[:, :, cols], hres[:, :, cols], two(ps[:, 4 + i, :]), ALU.add).then_inc(b_h, 1)
                dve.wait_ge(b_h, i + 1)
                dve.tensor_tensor(u[:, :, cols], hres[:, :, cols],
                                  ln2b[:, cols].unsqueeze(1).broadcast_to([P, NT, COLS]), ALU.mult).then_inc(n_u, 1)
            dve.wait_ge(b_h, 4)
            dve.memset(ps[:, 4, :], 0.0).then_inc(e_zero, 1)
            dve.memset(ps[:, 5, :], 0.0).then_inc(e_zero, 1)
            dve.memset(f32(selt[:, :, :]), 0.0).then_inc(e_back, 1)
            dve.memset(rinfo[:, :], 0.0).then_inc(n_init, 1)
            dve.memset(qsl[:, :, :], -1.0).then_inc(n_init, 1)
            dve.wait_ge(n_init, 2)
            dve.wait_ge(n_ss, 4 * NT)
            link(dve.tensor_reduce(stat[:, 0, 0:NT], stat[:, 5, 0:4 * NT].rearrange("p (i t) -> p t i", t=NT), AX_X,
                                   ALU.add))
            rsqrt(NT, 1.0 / D, None)
            R = [rt[:, i, :, :] for i in range(24)]
            io4 = iota[:, 0:4].unsqueeze(1).broadcast_to([P, NT, 4])

            def col(i):
                return rt[:, i, :, 0:1]

            def wide(i):
                return rt[:, i, :, 0:1].broadcast_to([P, NT, 4])

            def first_max(src, best, onehot, scratch):
                link(dve.tensor_reduce(col(best), R[src], AX_X, ALU.max))
                link(dve.tensor_tensor(R[scratch], R[src], wide(best), ALU.is_equal))
                link(dve.scalar_tensor_tensor(R[scratch], R[scratch], -16.0, io4, ALU.mult, ALU.add))
                link(dve.tensor_reduce(col(onehot), R[scratch], AX_X, ALU.min))
                link(dve.tensor_copy(col(scratch + 1), col(onehot)))
                link(dve.tensor_tensor(R[onehot], R[scratch], wide(scratch + 1), ALU.is_equal))

            def select(it):
                for t in range(NT):
                    ins = dve.tensor_scalar(sel[:, t, :], iota, qsl[:, t, bass.ds(it, 1)], None, ALU.is_equal)
                ins.then_inc(e_sel, 1)

            dve.wait_ge(n_log, 1)
            link(dve.tensor_tensor(rl[:, :, :], ps[:, 2:4, 0:20],
                                   stat[:, 1, 0:NT].unsqueeze(2).broadcast_to([P, NT, 20]), ALU.mult))
            link(dve.tensor_tensor(rl[:, :, :], rl[:, :, :],
                                   row[:, R_BG:R_END].unsqueeze(1).broadcast_to([P, NT, 20]), ALU.add))
            link(dve.tensor_copy(R[0], rl[:, :, 0:4]))
            first_max(0, 1, 2, 20)
            link(dve.tensor_tensor(R[12], rt[:, 2, 0, :].unsqueeze(1).broadcast_to([P, NT, 4]),
                                   rt[:, 2, 1, :].unsqueeze(1).broadcast_to([P, NT, 4]), ALU.add))
            dve.tensor_tensor(R[3], R[0], wide(1), ALU.subtract).then_inc(n_lg, 1)
            dve.wait_ge(n_ut, 4)
            for t in range(NT):
                dve.tensor_scalar(u[:, t, :], u[:, t, :], stat[:, 1, t:t + 1], None, ALU.mult).then_inc(n_u, 1)
            dve.wait_ge(n_cnt, 1)
            link(dve.tensor_tensor(R[23], ps[:, 2, 0:8].rearrange("p (t g) -> p t g", t=NT), R[2], ALU.mult))
            link(dve.tensor_scalar(qsl[:, :, 0:4], R[23], -1.0, None, ALU.add))
            select(0)
            link(dve.tensor_reduce(col(22), R[23], AX_X, ALU.add))
            link(dve.tensor_scalar(qsl[:, :, 4:5], col(22), -1.0 - P, None, ALU.add))
            link(dve.tensor_scalar(rinfo[:, 0:4], ps[:, 2, 8:12], float(P), None, ALU.is_gt))
            link(dve.tensor_reduce(rinfo[:, 4:5], rinfo[:, 0:4], AX_X, ALU.add))
            link(dve.tensor_scalar(rinfo[:, 6:7], rinfo[:, 4:5], float(GROUPS), None, ALU.add))
            link(dve.tensor_tensor(rinfo[:, 0:4], rinfo[:, 0:4], iota[:, 0:4], ALU.mult))
            link(dve.tensor_reduce(rinfo[:, 7:8], rinfo[:, 0:4], AX_X, ALU.add))
            dve.tensor_copy(rint[:, :], rinfo[:, 6:8]).then_inc(n_route, 1)
            grp = rl[:, :, 4:20].rearrange("p t (g e) -> p t g e", g=GROUPS)
            re4 = re[:, :, :].rearrange("p t (g e) -> p t g e", g=GROUPS)
            link(dve.tensor_tensor(re4, grp, R[2].unsqueeze(3).broadcast_to([P, NT, GROUPS, EXPERTS]), ALU.mult))
            link(dve.tensor_reduce(R[6], re[:, :, :].rearrange("p t (g e) -> p t e g", g=GROUPS), AX_X, ALU.add))
            first_max(6, 7, 8, 20)
            link(dve.scalar_tensor_tensor(R[9], R[8], -1e30, R[6], ALU.mult, ALU.add))
            first_max(9, 10, 11, 20)
            dve.tensor_tensor(col(15), col(10), col(7), ALU.subtract).then_inc(n_lg, 1)
            dve.wait_ge(n_exp, 2)
            link(dve.tensor_reduce(col(5), R[4], AX_X, ALU.add))
            link(dve.tensor_scalar(col(13), col(16), 1.0, None, ALU.add))
            link(dve.tensor_tensor(col(14), col(5), col(13), ALU.mult))
            link(dve.reciprocal(col(17), col(14)))
            link(dve.tensor_tensor(col(18), col(17), col(16), ALU.mult))
            link(dve.tensor_tensor(R[19], R[8], wide(17), ALU.mult))
            link(dve.tensor_tensor(R[20], R[11], wide(18), ALU.mult))
            dve.tensor_tensor(cw[:, :, :], R[19], R[20], ALU.add).then_inc(n_cw, 1)
            dve.wait_ge(n_route, 1)
            runs = dve.value_load(rint[0:1, 0:1], min_val=GROUPS, max_val=GROUPS + 1)

            def x_low(it):
                dve.wait_ge(e_cs, it + 1)
                dve.tensor_copy(cslot[:, :], ps[:, 7, 0:EXPERTS])
                dve.wait_ge(e_xhi, it + 1)
                dve.tensor_tensor(xg[:, 1, :, :].rearrange("p k s -> p (k s)"),
                                  ps[:, 0:2, :].rearrange("p a b -> p (a b)"),
                                  f32(xg[:, 0, :, :].rearrange("p k s -> p (k s)")), ALU.subtract).then_inc(e_xlo, 1)

            def y_low(it):
                dve.wait_ge(e_yhi, it + 1)
                dve.tensor_tensor(ysp[:, 1, :], ps[:, 4:6, :].rearrange("p a b -> p (a b)"), f32(ysp[:, 0, :]),
                                  ALU.subtract).then_inc(e_ylo, 1)

            def y_add_back(it, t):
                dve.wait_ge(e_scat, it * NT + (t + 1))
                dve.tensor_tensor(hres[:, t, :], hres[:, t, :],
                                  ps[:, 4:6, :].rearrange("p a b -> p (a b)"), ALU.add).then_inc(e_add, 1)

            with dve.Fori(0, runs) as it:
                def mlo(n):
                    dve.wait_ge(hi_done, it * MOE_PIECES + (N_MIX + n + 1))
                    dve.tensor_tensor(los[n % MOE_RING], mring[n % MOE_RING], f32(his[n % MOE_HI]),
                                      ALU.subtract).then_inc(lo_done, 1)

                mlo(0)
                x_low(it)
                mlo(1)
                y_low(it)
                mlo(2)
                dve.wait_ge(e_xlo, it + 1)
                for n, (kind, e, half) in enumerate(ORDER):
                    if n == SCATTER_0:
                        y_add_back(it, 0)
                        dve.wait_ge(e_add, it * 2 + 1)
                    if n == SCATTER_1:
                        y_add_back(it, 1)
                        dve.wait_ge(e_add, it * 2 + 2)
                    if n + 3 < MOE_PIECES:
                        mlo(n + 3)
                    if (kind, half) == ("up", 1):
                        dve.wait_ge(e_silu, it * EXPERTS + (e + 1))
                        dve.wait_ge(piece_mm, it * MOE_PIECES + (N_MIX + n + 1))
                        dve.scalar_tensor_tensor(hbuf[:, e % 2, :], sgate, cslot[:, e:e + 1],
                                                 ps[:, 2 * (e % 2) + 1, :], ALU.mult, ALU.mult).then_inc(e_h, 1)
                    if n + 1 in TURN_H:
                        d = TURN_H[n + 1]
                        dve.wait_ge(e_hthi, it * EXPERTS + (d + 1))
                        dve.tensor_tensor(ht[:, d % 2, 1, :, :].rearrange("p a b -> p (a b)"), ps[:, 6, :],
                                          f32(ht[:, d % 2, 0, :, :].rearrange("p a b -> p (a b)")),
                                          ALU.subtract).then_inc(e_htlo, 1)
                    if n == TURN_SEL:
                        dve.wait_ge(e_turn, it + 1)
                        dve.wait_ge(e_gath, it + 1)
                        select(it + 1)
            y_low(runs)
            for t in range(NT):
                y_add_back(runs, t)

            dve.wait_ge(f_ss, NT)
            dve.wait_ge(s_fin, 16)
            rsqrt(NT, 1.0 / D, None)
            for t in range(NT):
                dve.scalar_tensor_tensor(u[:, t, :], hres[:, t, :], stat[:, 1, t:t + 1], finb[:, :],
                                         ALU.mult, ALU.mult).then_inc(f_out, 1)

        @block.gpsimd
        def _(pool):
            pool.memset(heads16[:, :], 0.0).then_inc(sq_done, 1)
            pool.wait_ge(sq_done, 1)
            pool.memset(heads16[:, 15:16], 1.0).then_inc(sq_done, 1)
            pool.wait_ge(xt_mm, 4)
            for i in range(8):
                pool.wait_ge(silu_done, i + 1)
                src = cv[:, 2 * i:2 * i + 2, :].rearrange("p a b -> p (a b)")
                pool.tensor_tensor(sq[:, i * 512:(i + 1) * 512], src, src, ALU.mult).then_inc(sq_done, 1)
            pool.wait_ge(evac_a, 12 + 2)
            pool.wait_ge(s_cst, 32)
            pool.wait_ge(s_tab, 32)
            pool.wait_ge(dec_v, 1)
            log_decays = (f32(vdec_h[:, :, :]), vdec_l[:, :, :])

            def same(dst, src):
                one = ones[:, 0:1]
                for d in range(len(src.shape) - 2):
                    one = one.unsqueeze(1)
                return pool.tensor_tensor(dst, src, one.broadcast_to(list(src.shape)), ALU.mult)

            def stage(it):
                same(kq_h, kqt[:, bass.ds(it * 2, 2), :].rearrange("p a b -> p (a b)"))\
                    .then_inc(g_staged, 1)
                for part, v in enumerate(log_decays):
                    for h in range(2):
                        for c in range(NT):
                            n = 2 * h + c
                            ins = pool.tensor_tensor(
                                gdnrhs[:, part, n * P:(n + 1) * P], causal,
                                v[:, c, bass.ds(it * 2 + (SSD_HEADS + h), 1)].broadcast_to([P, P]), ALU.mult)
                ins.then_inc(g_rhs, 1)

            def ssd_rhs(it, k):
                for part, v in enumerate(log_decays):
                    pool.tensor_tensor(ssdrhs[:, k % 2, part, 0:256], causal2,
                                       v[:, 0, bass.ds(it * 8 + k, 1)].broadcast_to([P, 256]), ALU.mult)
                    ins = pool.tensor_tensor(ssdrhs[:, k % 2, part, 256:384], causal,
                                             v[:, 1, bass.ds(it * 8 + k, 1)].broadcast_to([P, P]), ALU.mult)
                ins.then_inc(m_rhs, 1)

            def iteration(it, ahead):
                def direct(k):
                    for t in range(NT):
                        ins = pool.tensor_tensor(
                            xd[:, t, :, :],
                            xy[:, t, bass.ds(it * 512 + k * 256, 256)].rearrange("p (h d) -> p h d", h=4),
                            row[:, bass.ds(it * 8 + (R_D + 4 * k), 4)].unsqueeze(2).broadcast_to([P, 4, SSD_HD]),
                            ALU.mult)
                    ins.then_inc(m_xd, 1)

                pool.wait_ge(g_oadd, it + 1)
                for dst in (inv, invt):
                    same(four(dst), ident.unsqueeze(1).broadcast_to([P, 4, P])).then_inc(g_eye, 1)
                pool.wait_ge(g_exp, it + 1)
                pool.tensor_tensor(four(gdecm[:, :]), four(gdec[:, :]), causal.unsqueeze(1).broadcast_to([P, 4, P]),
                                   ALU.mult).then_inc(g_mask, 1)
                direct(0)
                for k in range(2, 8):
                    pool.wait_ge(m_seg, it * 8 + (k - 1))
                    ssd_rhs(it, k)
                pool.wait_ge(g_staged, it + 1)
                same(kq_t[:, :, :], kq_h.rearrange("p (h c n) -> p h c n", h=2, c=NT)[:, :, 1, :])\
                    .then_inc(g_tail, 1)
                pool.wait_ge(m_ydone, it * 2 + 1)
                direct(1)
                if ahead:
                    pool.wait_ge(g_kq, it + 1)
                    pool.wait_ge(g_seg, it + 1)
                    pool.wait_ge(g_tail, it + 1)
                    stage(it + 1)
                    for k in (0, 1):
                        pool.wait_ge(m_seg, it * 8 + (7 + k))
                        ssd_rhs(it + 1, k)
                pool.wait_ge(m_ydone, it * 2 + 2)

            stage(0)
            ssd_rhs(0, 0)
            ssd_rhs(0, 1)
            with pool.Fori(0, GDN_HEADS // 2 - 1) as it:
                iteration(it, True)
            iteration(GDN_HEADS // 2 - 1, False)

            for t in range(NT):
                pool.tensor_tensor(xy[:, t, 0:1024], xy[:, t, 0:1024], z[:, t, 0:1024], ALU.mult).then_inc(b_yz, 1)
            pool.wait_ge(b_red, 1)
            pool.wait_ge(g_oadd, GDN_HEADS // 2 + 1)
            for t in range(NT):
                ot = o[:, t, :].rearrange("p (h d) -> p h d", d=P)
                pool.tensor_tensor(ot, ot, orms[:, t * 8:(t + 1) * 8].unsqueeze(2).broadcast_to([P, 8, P]),
                                   ALU.mult).then_inc(b_o, 1)
            pool.wait_ge(b_zs, 1)
            for t in range(NT):
                pool.wait_ge(b_o, t + 1)
                ot = o[:, t, :].rearrange("p (i c) -> p i c", i=4)
                pool.tensor_tensor(ot, ot, zg[:, :, t, :], ALU.mult).then_inc(b_o, 1)

        @block.tensor
        def _(pe):
            def triple(dst, w_hi, w_lo, a_hi, a_lo, start, stop, stationary):
                if stationary == "w":
                    pe.matmul(dst, w_hi, a_hi, start=start, stop=False)
                    pe.matmul(dst, w_hi, a_lo, start=False, stop=False)
                    return pe.matmul(dst, w_lo, a_hi, start=False, stop=stop)
                pe.matmul(dst, a_hi, w_hi, start=start, stop=False)
                pe.matmul(dst, a_hi, w_lo, start=False, stop=False)
                return pe.matmul(dst, a_lo, w_hi, start=False, stop=stop)

            def cm_step(p, m, k, dst, a, start, stop, slots=2):
                h, l = parts(p, slots)
                cols = slice(m * P, (m + 1) * P)
                return triple(dst, h[:, k, cols], l[:, k, cols], a[0], a[1], start, stop, "w")

            def tm_step(p, t, k, dst, start, stop):
                h, l = parts(p, 2)
                toks = slice(t * P, (t + 1) * P)
                return triple(dst, h[:, k, :], l[:, k, :], act_r[:, 0, k, toks], act_r[:, 1, k, toks], start, stop,
                              "a")

            def parts(p, slots):
                high = back_his[(p - P_WSSD) % 3] if slots == 3 else his[p % slots]
                views = (high, los[p % RING])
                return [v.rearrange("p (k c) -> p k c", k=KC) for v in views]

            def keep_warm(n):
                for _ in range(n):
                    pe.matmul(ps[:, 6, :], ident, cst[:, 0:512], start=True, stop=True)

            pe.wait_ge(s_cst, 32)
            keep_warm(3)
            for t in range(NT):
                pe.wait_ge(xn_done, t + 1)
            for b in range(4):
                for k in (2 * b, 2 * b + 1):
                    for t in range(NT):
                        ins = pe.transpose(ps[:, 2 + b, (k % 2) * SEQ + t * P:(k % 2) * SEQ + (t + 1) * P],
                                           xn[:, t, k * P:(k + 1) * P], ident)
                ins.then_inc(xt_mm, 1)
            def conv_piece(p, j):
                pe.wait_ge(lo_done, p + 1)
                if not (isinstance(p, int) and p < RING):
                    pe.wait_ge(tap_step, p * 6 - 18)
                for m in range(2):
                    for k in range(KC):
                        ins = cm_step(j, m, k, ps[:, j, m * SEQ:(m + 1) * SEQ], (act_r[:, 0, k, :], act_r[:, 1, k, :]),
                                      k == 0, k == KC - 1, RING)
                ins.then_inc(piece_mm, 1)

            keep_warm(4)
            pe.wait_ge(xt_lo, KC)
            for j in range(RING):
                conv_piece(j, j)
                if j == 0:
                    pe.wait_ge(sml_lo, 1)
                    for t in range(NT):
                        for k in range(KC):
                            w = slice(k * SMALL, (k + 1) * SMALL)
                            ins = triple(ps[:, 6, t * SMALL:(t + 1) * SMALL], sml_h[:, w], sml_l[:, w],
                                         act_r[:, 0, k, t * P:(t + 1) * P], act_r[:, 1, k, t * P:(t + 1) * P],
                                         k == 0, k == KC - 1, "a")
                    ins.then_inc(sml_mm, 1)
            with pe.Fori(1, N_CONV // RING) as q:
                for j in range(RING):
                    conv_piece(q * RING + j, j)

            def turn_fill(what, i, first_tile):
                f = fill_no[what, i]
                if f >= 5:
                    wait_evac(pe, f - 5)
                t, b = i % NT, i // NT
                for m in range(4):
                    ins = pe.transpose(bank(f)[:, m * P:(m + 1) * P],
                                       cv[:, first_tile + 4 * b + m, t * P:(t + 1) * P], ident)
                ins.then_inc(fill_mm, 1)

            pe.wait_ge(dec_v, 1)
            for t in range(NT):
                pe.matmul(ps[:, 6, t * 8:(t + 1) * 8], causal, vdec[:, t, SSD_HEADS:], start=True, stop=True)
            pe.matmul(ps[:, 6, 16:24], strict, vdec[:, 0, SSD_HEADS:], start=True, stop=True).then_inc(dec_mm, 1)
            pe.wait_ge(sq_done, 10)
            for c in range(16):
                ins = pe.matmul(ps[0:16, 7, 0:SEQ], heads16[:, 15 - c:31 - c], sq[:, c * SEQ:(c + 1) * SEQ],
                                start=(c == 0), stop=(c == 15))
            ins.then_inc(ss_mm, 1)
            pe.wait_ge(silu_done, N_CONV)
            def turn_piece(i):
                p = P_TURN + i
                pe.wait_ge(lo_done, p + 1)
                pe.wait_ge(acc_free, i + 1)
                for t in range(NT):
                    for k in range(KC):
                        ins = tm_step(p, t, k, ps[:, p % 2, t * SEQ:(t + 1) * SEQ], k == 0, k == KC - 1)
                ins.then_inc(piece_mm, 1)

            for i in range(4):
                turn_fill("v", i, 16)
            pe.wait_ge(ss_mm, 2)
            for t in range(NT):
                ins = pe.transpose(ps[:, 7, t * 16:(t + 1) * 16], ss16[0:16, t * P:(t + 1) * P], ident[0:16, 0:16])
            ins.then_inc(ss_mm, 1)
            turn_piece(0)
            pe.wait_ge(dec_tab, 2)
            for i in range(8):
                turn_fill("x", i, 24)
            for i in range(4):
                turn_fill("k", i, 8)
            turn_piece(1)
            for i in range(SSD_GROUPS):
                f = fill_no["cb", i]
                wait_evac(pe, f - 5)
                pe.matmul(bank(f)[:, 0:SEQ], cv[:, 40 + i, 0:P], cv[:, 44 + i, :], start=True, stop=True)
                pe.matmul(bank(f)[:, SEQ:SEQ + P], cv[:, 40 + i, P:SEQ], cv[:, 44 + i, P:SEQ],
                          start=True, stop=True).then_inc(fill_mm, 1)
            for i in range(4):
                turn_fill("q", i, 0)
            turn_piece(2)
            pe.wait_ge(evac_d, 12)
            for i in range(GDN_HEADS):
                f = fill_no["kqt", i]
                wait_evac(pe, f - 5)
                for c in range(NT):
                    kk = ktok[:, i * P:(i + 1) * P] if c == 0 else knorm1[:, i * P:(i + 1) * P]
                    pe.transpose(bank(f)[:, c * 256:c * 256 + P], kk, ident)
                    ins = pe.transpose(bank(f)[:, c * 256 + P:(c + 1) * 256], qn[:, c, i * P:(i + 1) * P], ident)
                ins.then_inc(fill_mm, 1)
            turn_piece(3)
            pe.wait_ge(evac_a, 12 + GDN_HEADS)
            pe.wait_ge(tab_done, 2)
            pe.wait_ge(cst_r, 3)

            with pe.Fori(0, GDN_HEADS // 2) as it:
                done = [0]

                def stream(steps):
                    for _ in range(steps):
                        j, s = divmod(done[0], 16)
                        m, k = divmod(s, KC)
                        if s == 0:
                            pe.wait_ge(lo_done, it * 4 + (P_LOOP + j + 1))
                            pe.wait_ge(acc_free, it * 4 + (N_TURN + j + 1))
                        dst = ps[:, j % 2, m * SEQ:(m + 1) * SEQ]
                        if j % 2 == 0:
                            ins = tm_step(j, m, k, dst, k == 0, k == KC - 1)
                        else:
                            ins = cm_step(j, m, k, dst, (act_r[:, 0, k, :], act_r[:, 1, k, :]), k == 0, k == KC - 1)
                        if s == 15:
                            ins.then_inc(piece_mm, 1)
                        done[0] += 1

                def segments(k):
                    pe.wait_ge(m_rhs, it * 8 + (k + 1))
                    if k >= 2:
                        pe.wait_ge(m_exp, it * 8 + (k - 1))
                    dst = ps[:, 5 + k % 2, :]
                    for part in range(2):
                        pe.matmul(dst[:, 0:384], strict_r[:, :], ssdrhs[:, k % 2, part, :], start=(part == 0),
                                  stop=False)
                    for part in range(2):
                        ins = pe.matmul(dst[:, P:2 * P], ones_r[:, :], ssdrhs[:, k % 2, part, 256:384], start=False,
                                        stop=(part == 1))
                    ins.then_inc(m_seg, 1)

                def ssd_out(k):
                    pe.wait_ge(m_gl, it * 8 + (k + 1))
                    if k == 4:
                        pe.wait_ge(m_ydone, it * 2 + 1)
                    c = (k % 4) * SSD_HD
                    xs = [xy[:, t, bass.ds(it * 512 + k * SSD_HD, SSD_HD)] for t in range(NT)]
                    pe.matmul(ps[:, 7, c:c + SSD_HD], ldec[:, k % 2, 0:P], xs[0], start=True, stop=True)
                    pe.matmul(ps[:, 7, 256 + c:256 + c + SSD_HD], ldec[:, k % 2, P:2 * P], xs[0], start=True,
                              stop=False)
                    pe.matmul(ps[:, 7, 256 + c:256 + c + SSD_HD], ldec[:, k % 2, 2 * P:3 * P], xs[1], start=False,
                              stop=True).then_inc(m_y, 1)

                def four_mm(b, lhs, rhs, done_sem):
                    for n in range(4):
                        c = slice(n * P, (n + 1) * P)
                        ins = pe.matmul(ps[:, b, c], lhs[:, c], rhs[:, c], start=True, stop=True)
                    ins.then_inc(done_sem, 1)

                pe.wait_ge(g_staged, it + 1)
                for h in range(2):
                    for c in range(NT):
                        a = (2 * h + c) * 256
                        ins = pe.matmul(ps[:, 2 + h, c * 256:(c + 1) * 256], kq_h[:, a:a + P], kq_h[:, a:a + 256],
                                        start=True, stop=True)
                ins.then_inc(g_kq, 1)
                pe.wait_ge(g_rhs, it + 1)
                pe.wait_ge(g_oadd, it + 1)
                for part in range(2):
                    ins = pe.matmul(ps[:, 4, :], strict_r[:, :], gdnrhs[:, part, :], start=(part == 0),
                                    stop=(part == 1))
                ins.then_inc(g_seg, 1)
                stream(4)
                segments(0)
                segments(1)
                stream(4)
                pe.wait_ge(g_nt, it + 1)
                for n in range(4):
                    ins = pe.transpose(ps[:, 4, n * P:(n + 1) * P], nmat[:, n * P:(n + 1) * P], ident)
                ins.then_inc(g_ntt, 1)
                stream(4)
                pe.wait_ge(g_aqk, it + 1)
                gaps = ((3, 0, 3), (3, 0, 3), (3, 0, 3), (3, 1, 1), (3, 2, 2), (3, 3, 0))
                for l, (after_p, before, after) in enumerate(gaps, 1):
                    pe.wait_ge(g_x, it * 6 + l)
                    four_mm(2, nmat, inv, g_p)
                    if l <= 4:
                        ssd_out(2 * l - 2)
                        if l <= 3:
                            segments(2 * l)
                    stream(after_p)
                    pe.wait_ge(g_ps, it * 6 + l)
                    pe.wait_ge(g_y, it * 7 + l)
                    four_mm(4, pmat, invt, g_yp)
                    if l <= 4:
                        ssd_out(2 * l - 1)
                        if l <= 3:
                            segments(2 * l + 1)
                    stream(before)
                    if l == 6:
                        break
                    pe.wait_ge(g_y, it * 7 + (l + 1))
                    for n in range(4):
                        ins = pe.transpose(ps[:, 3, n * P:(n + 1) * P], invt[:, n * P:(n + 1) * P], ident)
                    ins.then_inc(g_xp, 1)
                    stream(after)
                vt = [[vtok[:, c, bass.ds(it * 256 + h * P, P)] for h in range(2)] for c in range(NT)]
                pe.wait_ge(g_y, it * 7 + 7)
                for h in range(2):
                    ins = pe.matmul(ps[:, 2, h * P:(h + 1) * P], invt[:, 2 * h * P:(2 * h + 1) * P], vt[0][h],
                                    start=True, stop=True)
                ins.then_inc(g_solve, 1)
                stream(3)
                pe.wait_ge(g_vn, it * 2 + 1)
                pe.wait_ge(g_kd, it + 1)
                for h in range(2):
                    pe.matmul(ps[:, 3, h * P:(h + 1) * P], kd[:, h, :], vnew[:, 0, h, :], start=True, stop=True)
                    ins = pe.matmul(ps[:, 4, h * P:(h + 1) * P], aqk[:, 2 * h * P:(2 * h + 1) * P], vnew[:, 0, h, :],
                                    start=True, stop=True)
                ins.then_inc(g_state, 1)
                stream(3)
                pe.wait_ge(g_scopy, it + 1)
                pe.wait_ge(g_tail, it + 1)
                for h in range(2):
                    pe.matmul(ps[:, 2, h * P:(h + 1) * P], kq_t[:, h, 0:P], s1[:, h * P:(h + 1) * P],
                              start=True, stop=True)
                    ins = pe.matmul(ps[:, 3, h * P:(h + 1) * P], kq_t[:, h, P:2 * P], s1[:, h * P:(h + 1) * P],
                                    start=True, stop=True)
                ins.then_inc(g_ks, 1)
                stream(3)
                pe.wait_ge(g_r, it + 1)
                for h in range(2):
                    ins = pe.matmul(ps[:, 2, h * P:(h + 1) * P], invt[:, (2 * h + 1) * P:(2 * h + 2) * P],
                                    resid[:, h, :], start=True, stop=True)
                ins.then_inc(g_solve, 1)
                stream(4)
                pe.wait_ge(g_vn, it * 2 + 2)
                pe.wait_ge(g_ocopy, it + 1)
                for h in range(2):
                    ins = pe.matmul(ps[:, 4, h * P:(h + 1) * P], aqk[:, (2 * h + 1) * P:(2 * h + 2) * P],
                                    vnew[:, 1, h, :], start=True, stop=True)
                ins.then_inc(g_o1, 1)
                stream(3)
                assert done[0] == 64

            def back_fill(f):
                if 4 <= f < 9:
                    pe.wait_ge(bt_lo, f - 3 if f < 8 else 8)
                if f >= 9:
                    pe.wait_ge(b_m, 1 if f < 11 else 2)
                if f == 8:
                    for t in range(NT):
                        ins = pe.matmul(ps[:, back_bank[f], t * P:(t + 1) * P], ones, rdiag[:, t, :], start=True, stop=True)
                else:
                    for m in range(2):
                        for t in range(NT):
                            a = 2 * f + m if f < 8 else 2 * (f - 9) + m
                            src = xy if f < 8 else o
                            ins = pe.transpose(ps[:, back_bank[f], m * SEQ + t * P:m * SEQ + (t + 1) * P],
                                               src[:, t, a * P:(a + 1) * P], ident)
                ins.then_inc(bt_mm, 1)

            def ssd_piece(n):
                cb, half = SSD_ORDER[n]
                p = P_WSSD + n
                pe.wait_ge(lo_done, p + 1)
                for m in range(2):
                    for k in range(KC):
                        a = half * KC + k
                        if cb == 0 and m == 0 and k % 2 == 0:
                            pe.wait_ge(bt_lo, a // 2 + 1)
                        ins = cm_step(p, m, k, ps[:, SSD_BANKS[cb] + m, 0:SEQ],
                                      (yt[:, 0, a, :], yt[:, 1, a, :]), a == 0, a == 2 * KC - 1, 3)
                ins.then_inc(piece_mm, 1)

            pe.wait_ge(g_oadd, GDN_HEADS // 2 + 1)
            pe.wait_ge(acc_free, 2 + N_TURN + N_LOOP)
            pe.wait_ge(b_yz, NT)
            for f in range(4):
                back_fill(f)
            ssd_piece(0)
            pe.wait_ge(b_yz, 2 * NT)
            for f in range(4, 8):
                back_fill(f)
            ssd_piece(1)
            ssd_piece(2)
            ssd_piece(3)
            pe.wait_ge(b_rd, NT)
            back_fill(8)
            ssd_piece(4)
            ssd_piece(5)
            pe.wait_ge(b_o, 2 * NT)
            for f in range(9, 13):
                back_fill(f)
            pe.wait_ge(bt_lo, 9)
            ssd_piece(6)
            ssd_piece(7)
            pe.wait_ge(bt_lo, 13)
            for i in range(4):
                p = P_WGDN + i
                pe.wait_ge(lo_done, p + 1)
                for m in range(2):
                    for k in range(KC):
                        ins = cm_step(p, m, k, ps[:, i, m * SEQ:(m + 1) * SEQ],
                                      (act_r[:, 0, k, :], act_r[:, 1, k, :]), k == 0, k == KC - 1, 3)
                ins.then_inc(piece_mm, 1)
            def router_part(i):
                if i < 4:
                    pe.wait_ge(n_u, i + 1)
                    if i >= 2:
                        pe.wait_ge(n_utc, i - 1)
                    for m in range(2):
                        for t in range(NT):
                            a = 2 * i + m
                            ins = pe.transpose(ps[:, i % 2, m * SEQ + t * P:m * SEQ + (t + 1) * P],
                                               u[:, t, a * P:(a + 1) * P], ident)
                    ins.then_inc(n_ut, 1)
                if i >= 1:
                    pe.wait_ge(n_utc, i)
                    for k in (2 * i - 2, 2 * i - 1):
                        for t in range(NT):
                            ins = pe.matmul(ps[:, 2 + t, 0:20], ut[:, k, t * P:(t + 1) * P],
                                            wr[:, k * 20:(k + 1) * 20], start=(k == 0), stop=(k == KC - 1))
                    if i == 4:
                        ins.then_inc(n_log, 1)

            pe.wait_ge(b_m, 4)
            for i in range(4):
                p = P_WOUT + i
                pe.wait_ge(lo_done, p + 1)
                h, l = parts(p, 3)
                for t in range(NT):
                    for k in range(KC):
                        if i == 0 and t == 0 and k % 2 == 0:
                            pe.wait_ge(b_mlo, k // 2 + 1)
                        toks = slice(t * P, (t + 1) * P)
                        ins = triple(ps[:, 4 + i, t * SEQ:(t + 1) * SEQ], h[:, k, :], l[:, k, :],
                                     mt_r[:, 0, k, toks], mt_r[:, 1, k, toks], k == 0, k == KC - 1, "a")
                ins.then_inc(piece_mm, 1)
                if i == 1:
                    pe.wait_ge(b_m, 8)
                    pe.wait_ge(s_moep, 32)
                if i >= 1:
                    router_part(i - 1)
            router_part(3)
            keep_warm(1)
            router_part(4)
            keep_warm(6)
            pe.wait_ge(n_lg, 1)
            pe.matmul(ps[:, 2, 0:4], causal, rt[:, 2, 0, :], start=True, stop=True)
            pe.matmul(ps[:, 2, 4:8], ones, rt[:, 2, 0, :], start=True, stop=False)
            pe.matmul(ps[:, 2, 4:8], causal, rt[:, 2, 1, :], start=False, stop=True)
            pe.matmul(ps[:, 2, 8:12], ones, rt[:, 12, 0, :], start=True, stop=True).then_inc(n_cnt, 1)
            def gather(it):
                pe.wait_ge(e_sel, it + 1)
                for k in range(KC):
                    for t in range(NT):
                        ins = pe.matmul(ps[:, k // 4, (k % 4) * P:(k % 4 + 1) * P], u[:, t, k:D:KC], sel[:, t, :],
                                        start=(t == 0), stop=(t == 1))
                ins.then_inc(e_gath, 1)
                pe.wait_ge(n_cw, 1)
                for t in range(NT):
                    ins = pe.matmul(ps[:, 7, 0:EXPERTS], sel[:, t, :], cw[:, t, :], start=(t == 0), stop=(t == 1))
                ins.then_inc(e_cs, 1)

            def scatter(it, t):
                pe.wait_ge(e_yhi, it + 1)
                pe.wait_ge(e_ylo, it + 1)
                pe.wait_ge(e_back, it + 1)
                if t > 0:
                    pe.wait_ge(e_add, it * NT + t)
                for c in range(2):
                    for part in range(2):
                        ins = pe.matmul(ps[:, 4 + c, :], selt[:, t, :], ysp[:, part, c * 512:(c + 1) * 512],
                                        start=(part == 0), stop=(part == 1))
                ins.then_inc(e_scat, 1)

            pe.wait_ge(n_u, 4 + NT)
            gather(0)
            pe.wait_ge(n_route, 1)
            runs = pe.value_load(rint[0:1, 0:1], min_val=GROUPS, max_val=GROUPS + 1)
            keep_warm(3)
            with pe.Fori(0, runs) as it:
                pe.wait_ge(e_xhi, it + 1)
                pe.wait_ge(e_xlo, it + 1)
                for n, (kind, e, half) in enumerate(ORDER):
                    if n == SCATTER_0:
                        scatter(it, 0)
                    if n == SCATTER_1:
                        scatter(it, 1)
                    if n in TURN_H:
                        d = TURN_H[n]
                        pe.wait_ge(e_h, it * EXPERTS + (d + 1))
                        for f in range(4):
                            ins = pe.transpose(ps[:, 6, f * P:(f + 1) * P], hbuf[:, d % 2, f:FF:4], ident)
                        ins.then_inc(e_ht, 1)
                    if n == TURN_SEL:
                        for t in range(NT):
                            ins = pe.transpose(ps[:, 7, (t + 1) * P:(t + 2) * P], sel[:, t, :], ident)
                        ins.then_inc(e_turn, 1)
                    if n == NEXT_GROUP:
                        pe.wait_ge(e_back, it + 2)
                        with pe.If(it < runs - 1):
                            gather(it + 1)
                    if (kind, half) == ("down", 0):
                        pe.wait_ge(e_hthi, it * EXPERTS + (e + 1))
                        pe.wait_ge(e_htlo, it * EXPERTS + (e + 1))
                        if e == 0:
                            pe.wait_ge(e_add, it * NT + NT)
                    pe.wait_ge(lo_done, it * MOE_PIECES + (N_MIX + n + 1))
                    h, l = his[n % MOE_HI], los[n % MOE_RING]
                    if kind == "down":
                        for f in range(2):
                            for c in range(2):
                                w = slice(f * D + c * 512, f * D + (c + 1) * 512)
                                a = 2 * half + f
                                ins = triple(ps[:, 4 + c, :], h[:, w], l[:, w], ht[:, e % 2, 0, a, :],
                                             ht[:, e % 2, 1, a, :], e == 0 and a == 0, e == EXPERTS - 1 and a == 3,
                                             "a")
                    else:
                        for k in range(4):
                            w = slice(k * FF, (k + 1) * FF)
                            a = 4 * half + k
                            ins = triple(ps[:, 2 * (e % 2) + (kind == "up"), :], h[:, w], l[:, w], xg[:, 0, a, :],
                                         xg[:, 1, a, :], a == 0, a == KC - 1, "a")
                    ins.then_inc(piece_mm, 1)
            for t in range(NT):
                scatter(runs, t)


def constants():
    i = np.arange(P)
    causal = (i[:, None] <= i[None, :]).astype(np.float32)
    cst = np.concatenate([
        np.eye(P, dtype=np.float32), (i[:, None] > i[None, :]).astype(np.float32), causal,
        np.ones((P, P), np.float32), causal, np.tile(i.astype(np.float32), (P, 1))], axis=1)
    masks = np.zeros((P, 2, LEVELS, P), np.float32)
    for l in range(LEVELS):
        b = i >> l
        pair = (b[:, None] % 2 == 1) & (b[None, :] == b[:, None] - 1)
        masks[:, 0, l, :] = pair
        masks[:, 1, l, :] = pair.T
    return cst, masks.reshape(P, -1)


def cut_columns(w, halves=1):
    rows, cols = w.shape
    w = w.reshape(halves, KC, P, cols // COLS, COLS).transpose(3, 0, 2, 1, 4)
    return w.reshape(-1, P, PIECE)


def kernel(x, ln1_w, w_in, ssd_conv_w, ssd_conv_b, ssd_dt_bias, ssd_a_log, ssd_d, ssd_norm_w, w_ssd_proj,
           gdn_conv_w, gdn_dt_bias, gdn_a_log, gdn_norm_w, w_gdn_proj, b_merge, w_out, ln2_w,
           moe_w_group, moe_b_group, moe_w_expert, moe_b_expert, moe_w_gate, moe_w_up, moe_w_down,
           final_norm_w):
    import concourse.bacc as bacc
    from concourse.bass_utils import run_bass_kernel_spmd

    a = np.asarray
    w = a(w_in)[0]
    z_w, xbc_w, dt_w, qkv_w, ab_w, zg_w, gate_w = np.split(w, [2048, 5120, 5152, 8224, 8240, 9264], axis=1)
    zc, gc = cut_columns(z_w), cut_columns(gate_w)
    loop = np.stack([zc[4:], gc[0::2], cut_columns(zg_w), gc[1::2]], axis=1).reshape(-1, P, PIECE)
    ssd = cut_columns(a(w_ssd_proj)[0], 2)[[c * 2 + h for c, h in SSD_ORDER]]
    mix = np.concatenate([cut_columns(qkv_w), cut_columns(xbc_w), zc[:4], loop, ssd,
                          cut_columns(a(w_gdn_proj)[0]), cut_columns(a(w_out)[0])])
    small = np.concatenate([dt_w, ab_w], axis=1).reshape(KC, P, SMALL).transpose(1, 0, 2).reshape(P, KC * SMALL)
    conv = np.concatenate([a(gdn_conv_w)[0], a(ssd_conv_w)[0]], axis=1)
    bias = np.concatenate([np.zeros(3072, np.float32), a(ssd_conv_b)[0]])[None]
    conv = np.concatenate([conv, bias]).reshape(5, 48, P).transpose(2, 1, 0).reshape(P, 240)
    params = np.concatenate([conv, a(b_merge)[0].reshape(16, P).T, a(ln1_w)[0].reshape(KC, P).T,
                             a(ssd_norm_w)[0].reshape(16, P).T, a(gdn_norm_w)[0].reshape(1, P).T], axis=1)
    rows = np.concatenate([a(ssd_dt_bias)[0], a(gdn_dt_bias)[0], a(ssd_a_log)[0], a(gdn_a_log)[0], a(ssd_d)[0],
                           a(moe_b_group)[0], a(moe_b_expert)[0]])
    router = np.concatenate([a(moe_w_group)[0], a(moe_w_expert)[0]], axis=1)
    router = router.reshape(KC, P, 20).transpose(1, 0, 2).reshape(P, KC * 20)
    cst, masks = constants()
    arrays = {
        "w_mix": mix, "w_small": small, "w_router": router,
        "w_gate": a(moe_w_gate)[0].reshape(16, P, 2 * PIECE), "w_up": a(moe_w_up)[0].reshape(16, P, 2 * PIECE),
        "w_down": a(moe_w_down)[0].reshape(16, P, 2 * PIECE), "x": a(x), "consts": cst, "masks": masks,
        "params": params, "rows": rows, "ln2": a(ln2_w)[0], "final_w": a(final_norm_w),
    }
    arrays = {k: np.ascontiguousarray(v) for k, v in arrays.items()}
    nc = bacc.Bacc("TRN2", target_bir_lowering=False, num_devices=1)
    args = {k: nc.dram_tensor(k, v.shape, mybir.dt.from_np(v.dtype), kind="ExternalInput").ap()
            for k, v in arrays.items()}
    out = nc.dram_tensor("out", (1, SEQ, D), F32, kind="ExternalOutput").ap()
    hybrid_layer(nc, out=out, **args)
    r = run_bass_kernel_spmd(nc, [arrays], core_ids=[0])
    return r.results[0]["out"]
```
